# Optimizing a Trainium2 kernel written in Bass

```python
import math
import jax
import jax.numpy as jnp
from jax import lax
import numpy as np

D_MODEL = 2048
BATCH = 1
SEQ = 512
DEPTH = 1
DEC_BATCH = 8
DEC_SEQ = 8
PAST_LEN = 2048
PAGE_SIZE = 128

MIX_WIDTH = D_MODEL
ATTN_WIDTH = MIX_WIDTH // 2
CONV_DIM = MIX_WIDTH - ATTN_WIDTH
HEAD_DIM = 64
N_HEADS = ATTN_WIDTH // HEAD_DIM
KV_HEADS = 4
Q_PER_KV = N_HEADS // KV_HEADS
KV_WIDTH = KV_HEADS * HEAD_DIM
N_BRANCH = 3
BLOCK = 64
N_SEL = 16
WINDOW = 512
CONV_W = 3
D_FF = 4 * D_MODEL
ALPHA = (2.0 * DEPTH) ** 0.25
BETA = (8.0 * DEPTH) ** -0.25
LN_EPS = 1e-5
Q_BLOCK = 32
NEG = -1e30
FORCED_SCORE = 1e9
PROJ_SPLITS = (ATTN_WIDTH, 2 * KV_WIDTH, 2 * KV_WIDTH, 2 * KV_WIDTH, N_HEADS * N_BRANCH, CONV_DIM, CONV_DIM, CONV_DIM)
PROJ_WIDTH = sum(PROJ_SPLITS)

kernel_name = 'nsa_shortconv_hymba_deepnorm_step'

def layer_norm(x, g, b):
    xf = x.astype(jnp.float32)
    mu = jnp.mean(xf, axis=-1, keepdims=True)
    var = jnp.mean(jnp.square(xf - mu), axis=-1, keepdims=True)
    return ((xf - mu) * lax.rsqrt(var + LN_EPS) * g + b).astype(x.dtype)

def masked_softmax(s, mask):
    s = jnp.where(mask, s.astype(jnp.float32), NEG)
    m = jnp.max(s, axis=-1, keepdims=True)
    e = jnp.where(mask, jnp.exp(s - m), 0.0)
    return e / jnp.maximum(jnp.sum(e, axis=-1, keepdims=True), 1e-30)

def in_projection(h, w_in):
    u = jnp.einsum('btd,de->bte', h, w_in)
    B, T, _ = u.shape
    q, kv_c, kv_s, kv_w, g, xin, bg, cg = jnp.split(u, np.cumsum(PROJ_SPLITS)[:-1].tolist(), axis=-1)
    q = q.reshape(B, T, KV_HEADS, Q_PER_KV, HEAD_DIM)
    kv_c = kv_c.reshape(B, T, 2, KV_HEADS, HEAD_DIM)
    kv_s = kv_s.reshape(B, T, 2, KV_HEADS, HEAD_DIM)
    kv_w = kv_w.reshape(B, T, 2, KV_HEADS, HEAD_DIM)
    gates = jax.nn.sigmoid(g.reshape(B, T, KV_HEADS, Q_PER_KV, N_BRANCH))
    return q, kv_c, kv_s, kv_w, gates, xin, bg, cg

def nsa_attention(q, q_pos0, kv_cmp, kv_slc, kv_win, win_pos0, gates, w_cmp_k, w_cmp_v):
    B, Tq = q.shape[0], q.shape[1]
    L = kv_cmp.shape[1]
    scale = HEAD_DIM ** -0.5
    q_pos = q_pos0 + jnp.arange(Tq, dtype=jnp.int32)
    n_blk = -(-L // BLOCK)
    pad = n_blk * BLOCK - L
    blk = jnp.arange(n_blk, dtype=jnp.int32)
    pad_cfg = ((0, 0), (0, pad), (0, 0), (0, 0), (0, 0))
    kvc = jnp.pad(kv_cmp, pad_cfg).reshape(B, n_blk, BLOCK, 2, KV_HEADS, HEAD_DIM)
    k_cmp = jnp.einsum('bnlgd,ld->bngd', kvc[:, :, :, 0], w_cmp_k)
    v_cmp = jnp.einsum('bnlgd,ld->bngd', kvc[:, :, :, 1], w_cmp_v)
    s_c = jnp.einsum('bqgrd,bngd->bgrqn', q, k_cmp) * scale
    cmask = (blk[None, :] * BLOCK + BLOCK - 1) <= q_pos[:, None]
    p_c = masked_softmax(s_c, cmask)
    o_cmp = jnp.einsum('bgrqn,bngd->bqgrd', p_c.astype(v_cmp.dtype), v_cmp)
    cur = q_pos // BLOCK
    imp = jnp.sum(p_c, axis=2)
    forced = (blk[None, :] == 0) | (blk[None, :] == cur[:, None]) | (blk[None, :] == cur[:, None] - 1)
    cand = blk[None, :] <= cur[:, None]
    score = jnp.where(forced, FORCED_SCORE, jnp.where(cand, imp, -FORCED_SCORE))
    n_sel = min(N_SEL, n_blk)
    _, sel = lax.top_k(score, n_sel)
    qc = math.gcd(Tq, Q_BLOCK)
    n_chunk = Tq // qc
    kvs_blk = jnp.pad(kv_slc, pad_cfg).reshape(B, n_blk, BLOCK, 2, KV_HEADS, HEAD_DIM).transpose(0, 4, 1, 2, 3, 5)
    kvw_pad = jnp.pad(kv_win, ((0, 0), (WINDOW - 1, 0), (0, 0), (0, 0), (0, 0)))
    q_chunks = q.reshape(B, n_chunk, qc, KV_HEADS, Q_PER_KV, HEAD_DIM).swapaxes(0, 1)
    sel_chunks = sel.reshape(B, KV_HEADS, n_chunk, qc, n_sel).transpose(2, 0, 1, 3, 4)
    pos_chunks = q_pos.reshape(n_chunk, qc)
    b_idx = jnp.arange(B)[:, None, None, None]
    g_idx = jnp.arange(KV_HEADS)[None, :, None, None]
    offs = jnp.arange(BLOCK, dtype=jnp.int32)
    n_wk = WINDOW - 1 + qc
    w_offs = jnp.arange(n_wk, dtype=jnp.int32)

    def chunk_fn(args):
        qb, sb, pb = args
        kv_sel = kvs_blk[b_idx, g_idx, sb]
        k_pos = sb[..., None] * BLOCK + offs
        smask = (k_pos <= pb[None, None, :, None, None]).reshape(B, KV_HEADS, 1, qc, n_sel * BLOCK)
        s_s = jnp.einsum('bqgrd,bgqnkd->bgrqnk', qb, kv_sel[..., 0, :]) * scale
        p_s = masked_softmax(s_s.reshape(B, KV_HEADS, Q_PER_KV, qc, n_sel * BLOCK), smask)
        p_s = p_s.reshape(B, KV_HEADS, Q_PER_KV, qc, n_sel, BLOCK).astype(kv_sel.dtype)
        o_s = jnp.einsum('bgrqnk,bgqnkd->bqgrd', p_s, kv_sel[..., 1, :])
        start = pb[0] - win_pos0
        kvw = lax.dynamic_slice_in_dim(kvw_pad, start, n_wk, axis=1)
        w_pos = pb[0] - (WINDOW - 1) + w_offs
        delta = pb[:, None] - w_pos[None, :]
        wmask = (delta >= 0) & (delta < WINDOW) & (w_pos[None, :] >= win_pos0)
        s_w = jnp.einsum('bqgrd,bkgd->bgrqk', qb, kvw[:, :, 0]) * scale
        p_w = masked_softmax(s_w, wmask).astype(kvw.dtype)
        o_w = jnp.einsum('bgrqk,bkgd->bqgrd', p_w, kvw[:, :, 1])
        return o_s, o_w

    o_sel, o_win = lax.map(chunk_fn, (q_chunks, sel_chunks, pos_chunks))
    o_sel = o_sel.swapaxes(0, 1).reshape(B, Tq, KV_HEADS, Q_PER_KV, HEAD_DIM)
    o_win = o_win.swapaxes(0, 1).reshape(B, Tq, KV_HEADS, Q_PER_KV, HEAD_DIM)
    return gates[..., 0:1] * o_cmp + gates[..., 1:2] * o_sel + gates[..., 2:3] * o_win

def short_conv(xin, bg, cg, prev, conv_w):
    z = cg * xin
    T = z.shape[1]
    zp = jnp.concatenate([prev.astype(z.dtype), z], axis=1)
    y = conv_w[CONV_W - 1] * zp[:, CONV_W - 1:CONV_W - 1 + T]
    for j in range(CONV_W - 1):
        y = y + conv_w[j] * zp[:, j:j + T]
    return bg * y, zp[:, -(CONV_W - 1):]

def gather_pages(pool, page_table):
    pages = pool[page_table]
    return pages.reshape(page_table.shape[0], -1, *pool.shape[2:])

def hybrid_layer(x, past, w_in, w_cmp_k, w_cmp_v, conv_w, w_out, ln1_g, ln1_b, w_mlp1, w_mlp2, ln2_g, ln2_b):
    B, T, _ = x.shape
    q, kv_c, kv_s, kv_w, gates, xin, bg, cg = in_projection(x, w_in)
    if past is None:
        q_pos0 = 0
        kc_all, ks_all, kw_all = kv_c, kv_s, kv_w
        win_pos0 = 0
        conv_prev = jnp.zeros((B, CONV_W - 1, CONV_DIM), x.dtype)
        win_keep = min(WINDOW, T)
    else:
        pc, ps, pw, pconv = past
        q_pos0 = pc.shape[1]
        kc_all = jnp.concatenate([pc.astype(kv_c.dtype), kv_c], axis=1)
        ks_all = jnp.concatenate([ps.astype(kv_s.dtype), kv_s], axis=1)
        kw_all = jnp.concatenate([pw.astype(kv_w.dtype), kv_w], axis=1)
        win_pos0 = q_pos0 - pw.shape[1]
        conv_prev = pconv
        win_keep = pw.shape[1]
    attn = nsa_attention(q, q_pos0, kc_all, ks_all, kw_all, win_pos0, gates, w_cmp_k, w_cmp_v)
    conv_out, conv_state = short_conv(xin, bg, cg, conv_prev, conv_w)
    mix = jnp.einsum('bte,ed->btd', jnp.concatenate([attn.reshape(B, T, ATTN_WIDTH).astype(conv_out.dtype), conv_out], axis=-1), w_out)
    h = layer_norm(ALPHA * x + mix, ln1_g, ln1_b)
    f = jnp.einsum('btf,fd->btd', jnp.square(jax.nn.relu(jnp.einsum('btd,df->btf', h, w_mlp1))), w_mlp2)
    y = layer_norm(ALPHA * h + f, ln2_g, ln2_b)
    return y, kv_c, kv_s, kw_all[:, -win_keep:], conv_state

def setup_inputs(seed: int = 0) -> dict:
    key = jax.random.key(seed)
    ks = jax.random.split(key, 20)
    nrm = jax.random.normal
    f32 = jnp.float32
    n_pages = PAST_LEN // PAGE_SIZE
    n_pool = (DEC_BATCH * n_pages * 5) // 4
    win_buf = min(WINDOW, PAST_LEN)
    page_table = jax.random.permutation(ks[6], n_pool)[:DEC_BATCH * n_pages].reshape(DEC_BATCH, n_pages).astype(jnp.int32)
    return {
        'x_prompt': nrm(ks[0], (BATCH, SEQ, D_MODEL), f32),
        'x_sample': nrm(ks[1], (DEC_BATCH, DEC_SEQ, D_MODEL), f32),
        'cache_cmp': nrm(ks[2], (DEPTH, n_pool, PAGE_SIZE, 2, KV_HEADS, HEAD_DIM), f32),
        'cache_slc': nrm(ks[3], (DEPTH, n_pool, PAGE_SIZE, 2, KV_HEADS, HEAD_DIM), f32),
        'cache_win': nrm(ks[4], (DEPTH, DEC_BATCH, win_buf, 2, KV_HEADS, HEAD_DIM), f32),
        'state_conv': nrm(ks[5], (DEPTH, DEC_BATCH, CONV_W - 1, CONV_DIM), f32),
        'page_table': page_table,
        'w_in': nrm(ks[7], (DEPTH, D_MODEL, PROJ_WIDTH), f32) * D_MODEL ** -0.5,
        'w_cmp_k': (1.0 + 0.1 * nrm(ks[8], (DEPTH, BLOCK, HEAD_DIM), f32)) / BLOCK,
        'w_cmp_v': (1.0 + 0.1 * nrm(ks[9], (DEPTH, BLOCK, HEAD_DIM), f32)) / BLOCK,
        'conv_w': nrm(ks[10], (DEPTH, CONV_W, CONV_DIM), f32) * CONV_W ** -0.5,
        'w_out': nrm(ks[11], (DEPTH, MIX_WIDTH, D_MODEL), f32) * (MIX_WIDTH ** -0.5 * BETA),
        'ln1_g': 1.0 + 0.02 * nrm(ks[12], (DEPTH, D_MODEL), f32),
        'ln1_b': 0.02 * nrm(ks[13], (DEPTH, D_MODEL), f32),
        'w_mlp1': nrm(ks[14], (DEPTH, D_MODEL, D_FF), f32) * D_MODEL ** -0.5,
        'w_mlp2': nrm(ks[15], (DEPTH, D_FF, D_MODEL), f32) * (D_FF ** -0.5 * BETA),
        'ln2_g': 1.0 + 0.02 * nrm(ks[16], (DEPTH, D_MODEL), f32),
        'ln2_b': 0.02 * nrm(ks[17], (DEPTH, D_MODEL), f32),
    }

def reference(x_prompt, x_sample, cache_cmp, cache_slc, cache_win, state_conv, page_table, w_in, w_cmp_k, w_cmp_v, conv_w, w_out, ln1_g, ln1_b, w_mlp1, w_mlp2, ln2_g, ln2_b):
    yp, ys = x_prompt, x_sample
    cmp_p, slc_p, win_p, conv_p = [], [], [], []
    cmp_s, slc_s, win_s, conv_s = [], [], [], []
    for l in range(DEPTH):
        params = (w_in[l], w_cmp_k[l], w_cmp_v[l], conv_w[l], w_out[l], ln1_g[l], ln1_b[l], w_mlp1[l], w_mlp2[l], ln2_g[l], ln2_b[l])
        yp, c1, s1, w1, v1 = hybrid_layer(yp, None, *params)
        past = (gather_pages(cache_cmp[l], page_table), gather_pages(cache_slc[l], page_table), cache_win[l], state_conv[l])
        ys, c2, s2, w2, v2 = hybrid_layer(ys, past, *params)
        cmp_p.append(c1); slc_p.append(s1); win_p.append(w1); conv_p.append(v1)
        cmp_s.append(c2); slc_s.append(s2); win_s.append(w2); conv_s.append(v2)
    return (yp, ys, jnp.stack(cmp_p), jnp.stack(slc_p), jnp.stack(win_p), jnp.stack(conv_p), jnp.stack(cmp_s), jnp.stack(slc_s), jnp.stack(win_s), jnp.stack(conv_s))


_drawn_inputs = setup_inputs


def setup_inputs(seed=0):
    import zlib

    import numpy as np

    out = dict(_drawn_inputs(seed))
    spreads = {}
    factors = {'cache_cmp': 6.808,
     'cache_slc': 5.639,
     'w_cmp_k': 8.0,
     'w_cmp_v': 8.0,
     'ln1_g': 2.784,
     'ln1_b': 2.677,
     'ln2_g': 2.906,
     'ln2_b': 2.826}
    for name, (base, spread) in spreads.items():
        noise = np.random.default_rng([zlib.crc32(name.encode()), seed]).standard_normal(out[name].shape)
        drawn = base * np.exp(spread * noise) if base else spread * noise
        out[name] = jnp.asarray(drawn.astype(out[name].dtype))
    for name, factor in factors.items():
        out[name] = (out[name] * factor).astype(out[name].dtype)
    return out
```

```python
from contextlib import ExitStack

import numpy as np

import concourse.bass as bass
from concourse import mybir

ALU = mybir.AluOpType
ACT = mybir.ActivationFunctionType
AX = mybir.AxisListType
F32 = mybir.dt.float32
F32R = mybir.dt.float32r
I32 = mybir.dt.int32
U32 = mybir.dt.uint32

P = 128
D = 2048
TP = 512
NB, TS = 8, 8
TN = NB * TS
T = TP + TN
TH = T // 2
PAGE, NPAGE = 128, 16
PAST = PAGE * NPAGE
WIN = 512
HD = 64
G, R = 4, 4
BLK = 64
NBLK = PAST // BLK
PBLK = TP // BLK
NSEL = 16
FORCED = 3
CONV = 1024
FF = 8192
EPS = 1e-5
NEG = -1e30
SCALE = HD ** -0.5
ALPHA = 2.0 ** 0.25

KT = D // P
PT_TOK = TP // P
C_Q, C_KV, C_G, C_XIN = 0, 1024, 2560, 2608
C_BG, C_CG = C_XIN + CONV, C_XIN + 2 * CONV
NG = 3 * G * R
NKV = 12
KV_CMP, KV_SLC, KV_WIN = 0, 4, 8
NCONV = CONV // P

S_GATE = 0
S_CONV = 1
S_Q = S_CONV + 3 * NCONV
S_KV = S_Q + 8
S_OUT = S_KV + NKV
S_MLP = S_OUT + KT
CHUNK = 1024
NCHUNK = FF // CHUNK
CT = CHUNK // P
END = S_MLP + NCHUNK * 2 * CT
RAW_OUT_DMAS = 5

GROW = 8
GSEQ = P * GROW
NGATH = NB * PAST // GSEQ
UNITS = PT_TOK * G * R
ROWW = 2 * G * HD


class Names:
    pass


class Chain:

    def __init__(self, eng, sem):
        self.eng, self.sem, self.n, self.loop = eng, sem, 0, 0

    def __call__(self, ins):
        ins.then_inc(self.sem, 1)
        self.n += 1
        return self

    def wait(self):
        self.eng.wait_ge(self.sem, self.loop + self.n)

    def turns(self, count, per_turn):
        start, outer = self.n, self.loop
        with self.eng.Fori(0, count) as i:
            self.loop = outer + i * per_turn
            yield i
            assert self.n == start + per_turn, (self.n - start, per_turn)
        self.n, self.loop = start + per_turn * count, outer


DMAS = [2] * S_OUT + [RAW_OUT_DMAS] * KT + [2] * (END - S_MLP)


def raw_in(s, pairs=0):
    fixed = 16 * sum(DMAS[x] for x in range(s + 1) if x % 2 == s % 2)
    return fixed + pairs * (16 * DMAS[s])


def build(nc, x_prompt, x_sample, cache_cmp, cache_slc, cache_win, state_conv, page_table, w_in, w_cmp_k,
          w_cmp_v, conv_w, w_out, ln1_g, ln1_b, w_mlp1, w_mlp2, ln2_g, ln2_b,
          y_prompt, y_sample, new_cmp_prompt, new_slc_prompt, new_win_prompt, new_conv_prompt,
          new_cmp_sample, new_slc_sample, new_win_sample, new_conv_sample):
    ctx = ExitStack()
    with ctx:
        def sem(name):
            return ctx.enter_context(nc.semaphore(name))

        base = -(-nc.sbuf_base // 64) * 64
        W0 = base
        A0 = W0 + 6 * 8192
        B0 = A0 + 2 * KT * T * 4
        C0 = B0 + (8 + NKV) * T * 4
        K0 = C0 + KT * T * 4
        fixed = [K0]

        def at(name, offset, shape, dt=F32):
            return nc.alloc_sbuf_tensor_at(name, shape, dt, offset=offset)

        def const(name, shape, dt=F32):
            t = at(name, fixed[0], shape, dt)
            fixed[0] += -(-int(np.prod(shape[1:])) * 4 // 32) * 32
            assert fixed[0] <= nc.sbuf_usable_end, (name, fixed[0], nc.sbuf_usable_end)
            return t

        w_raw = [at(f"w_raw{i}", W0 + 8192 * i, [P, 2048]) for i in range(2)]
        w_hi = [at(f"w_hi{i}", W0 + 8192 * (2 + i), [P, 2048], F32R) for i in range(2)]
        w_lo = [at(f"w_lo{i}", W0 + 8192 * (4 + i), [P, 2048], F32R) for i in range(2)]
        x_hi = at("x_hi", A0, [P, KT, T], F32R)
        x_lo = at("x_lo", A0 + KT * T * 4, [P, KT, T], F32R)
        x_rows = at("x_rows", B0, [P, PT_TOK + 1, D])
        gath = [at(f"gath{i}", B0 + 16384 * i, [P, GROW, ROWW]) for i in range(2)]
        wcmp = at("wcmp", B0 + 32768, [P, 2, GROW, HD])
        part = [at(f"part{i}", B0 + 36864 + 2048 * i, [P, ROWW]) for i in range(2)]
        q_t = at("q_t", B0, [P, R, 2, T])
        kv_t = at("kv_t", B0 + 8 * T * 4, [P, NKV, T])
        x_t = at("x_t", C0, [P, KT, T])
        mix = at("mix", C0, [P, KT, T])
        xin = at("xin", C0, [P, T])
        ZW = 2 + TP + NB * (2 + TS)
        zpad = at("zpad", C0 + 2304, [P, ZW])
        fir = at("fir", C0 + 4736, [P, ZW])
        cmp_t0 = at("cmp_t0", C0 + 7168, [P, NB, 4, NBLK])
        gates0 = at("gates0", C0 + 11264, [P, T])
        st_in = at("st_in", A0, [2 * NB, CONV])
        zl_rows = at("zl_rows", C0, [2 + 2 * NB, CONV])

        kvn = at("kvn", W0, [P, PT_TOK + 1, NKV * P])
        qbd = at("qbd", W0 + 30720, [P, NB, 2, P])
        cmp_t = at("cmp_t", W0 + 38912, [P, NB, 4, NBLK])
        causal = at("causal", W0 + 43008, [P, 2 * TP - P])
        same = at("same", W0 + 46592, [P, P])
        tok_of = at("tok_of", W0 + 47104, [P, TS])
        grp_of = at("grp_of", W0 + 47136, [P, G])
        pair_of = at("pair_of", W0 + 47168, [P, 2 * R * 2])
        before = at("before", W0 + 47232, [P, TS])
        gn = at("gn", W0 + 47264, [P, PT_TOK, NG])
        gs = at("gs", W0 + 48032, [P, 3, NB])
        mb = at("mb", W0 + 48128, [P, NB, NBLK])
        nmask = at("nmask", W0 + 49152, [P, 2, TS])
        wmask = at("wmask", W0 + 49216, [P, TP])
        kn = at("kn", W0 + 51264, [P, 2, 2, TN])
        X0 = W0 + 53312
        tri = at("tri", X0, [P, P // TS, TS])
        gexp = at("gexp", X0 + 512, [NG, 3, P])
        gtmp = at("gtmp", X0 + 2048, [P, 3, TN])
        tmp = [at(f"tmp{i}", X0 + 3072 + 4096 * i, [P, 2, PBLK, BLK]) for i in range(2)]
        kc = at("kc", X0 + 11264, [P, 4, PBLK])
        kbd = at("kbd", X0 + 11392, [P, 2, 2 * PBLK])
        e8 = at("e8", X0 + 11520, [PBLK, P])
        vcn = at("vcn", X0 + 12032, [PBLK, G * HD])
        vrep = at("vrep", X0 + 13056, [P, G * HD])
        vbd = at("vbd", X0 + 14080, [P, 2 * R, P])
        sc = at("sc", X0 + 18176, [P, PT_TOK, P])
        cbias = at("cbias", X0 + 20224, [P, PT_TOK, PBLK])
        st1 = at("st1", X0 + 20352, [P, PT_TOK * 16])
        st2 = at("st2", X0 + 20608, [P, PT_TOK * 16])
        pct = at("pct", X0 + 20864, [P, TP])
        ss = at("ss", X0 + 22912, [P, NB, NBLK])
        pg = at("pg", X0 + 23936, [P, NB, NBLK])
        vals = at("vals", X0 + 24960, [P, NB, 40])
        m8 = at("m8", X0 + 26240, [P, 8])
        m5 = at("m5", X0 + 26272, [P, 8])
        st3 = at("st3", X0 + 26304, [P, NB])
        st4 = at("st4", X0 + 26336, [P, NB])
        pcts = at("pcts", X0 + 26368, [NBLK, NB, P])
        vcs = at("vcs", X0 + 30464, [NBLK, NB, 2, P])
        zero = at("zero", X0 + 38656, [P, TP])
        pS = [at(f"pS{i}", X0 + 4096 * i, [P, 2, TP]) for i in range(4)]
        pT = [at(f"pT{i}", X0 + 16384 + 4096 * i, [P, 8, P]) for i in range(2)]
        pq = [at(f"pq{i}", X0 + 24576 + 2048 * i, [P, TP]) for i in range(2)]
        pst = [at(f"pst{i}", X0 + 28672 + 64 * i, [P, 3, 2]) for i in range(4)]
        NS_COLS = PAST + TS + WIN + TS
        sg = [at(f"sg{i}", X0 + 16384 * i, [P, GROW, ROWW]) for i in range(4)]
        assert X0 + 65536 <= B0
        wb = [at(f"wb{i}", W0 + 8192 * i, [P, WIN // P, ROWW]) for i in range(2)]
        sS = [at("sS0", W0 + 16384, [P, NS_COLS]), at("sS1", B0, [P, NS_COLS])]
        vn = [at(f"vn{i}", B0 + 10304 + 2048 * i, [TS, 2, G * HD]) for i in range(2)]
        kT = [at(f"kT{i}", B0 + 14400 + 4096 * i, [P, 2, 512]) for i in range(2)]
        NPB = 22
        sT = at("sT", B0 + 22592, [P, NPB, P])
        sq_ = [at(f"qb{i}", B0 + 33856 + 1024 * i, [P, 2, P]) for i in range(2)]
        sst = [at(f"sst{i}", B0 + 35904 + 64 * i, [P, 3, 2]) for i in range(2)]
        mix_hi = at("mix_hi", A0, [P, KT, T], F32R)
        mix_lo = at("mix_lo", A0 + KT * T * 4, [P, KT, T], F32R)
        h_hi = at("h_hi", A0, [P, KT, T], F32R)
        h_lo = at("h_lo", A0 + KT * T * 4, [P, KT, T], F32R)
        x_r = at("x_r", B0, [P, KT, T])
        h_t = at("h_t", C0, [P, KT, T])
        f_hi = at("f_hi", B0, [P, CT, T], F32R)
        f_lo = at("f_lo", B0 + CT * T * 4, [P, CT, T], F32R)
        Y0 = B0 + KT * T * 4
        sqr = [at(f"sqr{i}", Y0 + 2304 * i, [P, T]) for i in range(2)]
        rstd = at("rstd", Y0 + 4608, [P, T])
        rl = [at(f"rl{i}", Y0 + 2304 * i, [P, T]) for i in range(2)]
        fs = [at(f"fs{i}", Y0 + 4608 + 2304 * i, [P, T]) for i in range(2)]
        o_rows = [at(f"o_rows{i}", A0 + 8192 * i, [P, D]) for i in range(PT_TOK + 1)]

        ident = const("ident", [P, P])
        means = const("means", [P, P])
        sel8 = const("sel8", [P, P // GROW])
        pars = const("pars", [88, P])
        pars_t = const("pars_t", [P, 88])
        st_t = const("st_t", [P, NCONV, NB, 2])
        zlast = const("zlast", [P, NCONV, 2 + 2 * NB])
        pt_i = const("pt_i", [NPAGE // 2, 2 * NB], I32)
        pt_f = const("pt_f", [NPAGE // 2, 2 * NB])
        w_of = const("w_of", [NPAGE // 2, 1])
        spread = const("spread", [NPAGE // 2, P])
        p_of = const("p_of", [P, 1])
        idx = const("idx", [P, NGATH], U32)
        idx1 = [const(f"idx1{i}", [P, 1], U32) for i in range(4)]
        w_rows = at("w_rows", A0 + 4096, [BLK, 4 * HD])
        wt = const("wt", [P, 2, BLK])
        LN1G, LN1B, LN2G, LN2B, CW = 0, KT, 2 * KT, 3 * KT, 4 * KT

        ps = ctx.enter_context(nc.psum_tensor("ps", [P, 8, 512], F32))

        def banks(a, n, cols):
            return ps[:, a:a + n, 0:cols]

        def flat(a, cols, rows=P):
            return ps[0:rows, a:a + 2, :].rearrange("p b c -> p (b c)")[:, 0:cols]

        x_dram = nc.dram_tensor("x_scratch", [P, KT * T], F32).ap()
        cmp_rows = cache_cmp.rearrange("o n (s j) c g d -> (o n s) (j c g d)", j=GROW)
        slc_rows = cache_slc.rearrange("o n (s j) c g d -> (o n s) (j c g d)", j=GROW)
        w_in_v = w_in[0].rearrange("(kt p) n -> p kt n", p=P)
        w_q_v = w_in[0][:, C_Q:C_Q + 1024].rearrange("(kt p) (a gl r d) -> p kt a gl r d", p=P, a=2, gl=2, r=R)

        s_par = sem("s_par")
        s_x = [sem(f"s_x{t}") for t in range(PT_TOK + 1)]
        s_asked, s_wcmp, s_pt, s_idx = sem("s_asked"), sem("s_wcmp"), sem("s_pt"), sem("s_idx")
        s_const = sem("s_const")
        s_idxs = sem("s_idxs")
        s_w = [sem(f"s_w{i}") for i in range(2)]
        s_hi, s_lo, s_gemm, s_acc = sem("s_hi"), sem("s_lo"), sem("s_gemm"), sem("s_acc")
        s_tr, s_trv = sem("s_tr"), sem("s_trv")
        s_pre, s_prev = sem("s_pre"), sem("s_prev")
        s_xt, s_xhi, s_xlo, s_xsave = sem("s_xt"), sem("s_xhi"), sem("s_xlo"), sem("s_xsave")
        s_gath = [sem(f"s_gath{i}") for i in range(2)]
        s_idx1, s_gfree, s_part, s_sel, s_cmpv = sem("s_idx1"), sem("s_gfree"), sem("s_part"), sem("s_sel"), sem("s_cmpv")
        s_gate = sem("s_gate")
        s_wr, s_wcopy = sem("s_wr"), sem("s_wcopy")
        s_kvT, s_kvn, s_kvout = sem("s_kvT"), sem("s_kvn"), sem("s_kvout")
        s_one, s_b, s_a = sem("s_one"), sem("s_b"), sem("s_a")
        s_mask = sem("s_mask")
        s_q, s_qk, s_mx, s_ex, s_sc, s_pt_, s_pe, s_pv, s_of = (sem(n) for n in
            ("s_q", "s_qk", "s_mx", "s_ex", "s_sc", "s_ptr", "s_pe", "s_pv", "s_of"))
        s_sg = [sem(f"s_sg{i}") for i in range(4)]
        s_wb, s_vn = [sem(f"s_wb{i}") for i in range(2)], [sem(f"s_vn{i}") for i in range(2)]
        t_i, t_qb, t_kt, t_ke, t_qk, t_se, t_mx, t_ex, t_sc, t_pt, t_pe, t_pv, t_of = (sem(n) for n in
            ("t_i", "t_qb", "t_kt", "t_ke", "t_qk", "t_se", "t_mx", "t_ex", "t_sc", "t_pt", "t_pe", "t_pv", "t_of"))
        s_mhi, s_mlo, s_xr, s_res = sem("s_mhi"), sem("s_mlo"), sem("s_xr"), sem("s_res")
        l_mean, l_sub, l_sq, l_acc, l_eps, l_sd, l_mul, l_aff, l_hi, l_lo = (sem(n) for n in
            ("l_mean", "l_sub", "l_sq", "l_acc", "l_eps", "l_sd", "l_mul", "l_aff", "l_hi", "l_lo"))
        l_al = sem("l_al")
        f_rl, f_f, f_h, f_l = sem("f_rl"), sem("f_f"), sem("f_h"), sem("f_l")
        o_tr, o_cp = sem("o_tr"), sem("o_cp")
        s_dve, s_act, s_pool = sem("s_dve"), sem("s_act"), sem("s_pool")
        s_zl, s_zlT, s_zlv, s_out = sem("s_zl"), sem("s_zlT"), sem("s_zlv"), sem("s_out")

        block = ctx.enter_context(nc.Block())

        @block.sync
        def _(sp):
            for row, ap in ((LN1G, ln1_g), (LN1B, ln1_b), (LN2G, ln2_g), (LN2B, ln2_b)):
                sp.dma_start(pars[row:row + KT, :], ap.rearrange("o (k p) -> (o k) p", p=P)).then_inc(s_par, 16)
            sp.dma_start(pars[CW:CW + 3 * NCONV, :], conv_w.rearrange("o j (c p) -> (o j c) p", p=P)).then_inc(s_par, 16)
            sp.dma_start(st_in[:, :], state_conv.rearrange("o b j n -> (o b j) n")).then_inc(s_par, 16)
            sp.dma_start(pt_i[:, :], page_table.rearrange("b (h w) -> w (b h)", w=NPAGE // 2),
                         allow_slow_non_contiguous=True).then_inc(s_par, 16)
            for m in range(4):
                sp.dma_start(w_rows[:, m * HD:(m + 1) * HD], (w_cmp_k, w_cmp_v)[m // 2][0]).then_inc(s_wr, 16)
            for t in range(PT_TOK):
                sp.dma_start(x_rows[:, t, :], x_prompt[0, t * P:(t + 1) * P, :]).then_inc(s_x[t], 16)
            sp.dma_start(x_rows[0:TN, PT_TOK, :], x_sample.rearrange("b t d -> (b t) d")).then_inc(s_x[PT_TOK], 16)

            def load(s, halves, it=0):
                if s >= 2 or not isinstance(it, int):
                    sp.wait_ge(s_lo, s - 1 + it)
                for dst, src in halves:
                    sp.dma_start(dst, src).then_inc(s_w[s % 2], 16)

            def by_k(s, src):
                _, kt, n = src.shape
                dst = w_raw[s % 2][:, :].rearrange("p (k n) -> p k n", n=n)
                return [(dst[:, h:h + kt // 2, :], src[:, h:h + kt // 2, :]) for h in (0, kt // 2)]

            def q_halves(s, a, r):
                dst = w_raw[s % 2][:, :].rearrange("p (k gl n) -> p k gl n", gl=2, n=HD)
                return [(dst[:, :, gl, :], w_q_v[:, :, a, gl, r, :]) for gl in range(2)]

            def conv_cols(u, c):
                return w_in_v[:, :, bass.ds((C_XIN, C_CG, C_BG)[u] + c * P, P)]

            load(S_GATE, by_k(0, w_in_v[:, :, C_G:C_G + P]))
            load(S_CONV, by_k(1, conv_cols(0, 0)))
            keep_rows = WIN - TS
            sp.dma_start(new_win_sample[0].rearrange("b (x y) c g d -> x b (y c g d)", y=4)[0:keep_rows // 4],
                         cache_win[0].rearrange("b (x y) c g d -> x b (y c g d)", y=4)[TS // 4:WIN // 4]).then_inc(s_out, 16)
            sp.wait_ge(s_tr, KT)
            for m, wc in enumerate((w_cmp_k, w_cmp_v)):
                sp.dma_start(wcmp[:, m, :, :].rearrange("p j d -> p (j d)"),
                             wc[0].rearrange("(s j) d -> s (j d)", s=GROW).unsqueeze(0).broadcast_to([P // GROW, GROW, GROW * HD])
                             ).then_inc(s_wcmp, 16)
            sp.wait_ge(s_xt, KT)
            sp.dma_start(x_dram, x_t[:, :, :].rearrange("p k t -> p (k t)")).then_inc(s_xsave, 16)
            sp.wait_ge(s_xsave, 16)
            sp.wait_ge(s_xhi, KT)
            sp.wait_ge(s_xlo, KT)
            for u in range(1, 6):
                load(S_CONV + u, by_k(S_CONV + u, conv_cols(u % 3, u // 3)))
            with sp.Fori(1, NCONV // 2) as i:
                for u in range(6):
                    load(S_CONV + u, by_k(S_CONV + u, conv_cols(u % 3, 2 * i + u // 3)), it=6 * i)
            with sp.Fori(0, R) as r:
                for a in range(2):
                    load(S_Q + a, q_halves(S_Q + a, a, r), it=2 * r)
            with sp.Fori(0, NKV // 2) as i:
                for u in range(2):
                    load(S_KV + u, by_k(S_KV + u, w_in_v[:, :, bass.ds(C_KV + u * P + i * (2 * P), P)]), it=2 * i)

            sp.wait_ge(s_zlv, 1)
            sp.dma_start(new_conv_prompt.rearrange("o b j n -> (o b j) n"), zl_rows[0:2, :]).then_inc(s_out, 16)
            sp.dma_start(new_conv_sample.rearrange("o b j n -> (o b j) n"), zl_rows[2:2 + 2 * NB, :]).then_inc(s_out, 16)
            for t in range(PT_TOK):
                sp.wait_ge(s_kvn, t + 1)
                for m, out in ((KV_CMP, new_cmp_prompt), (KV_SLC, new_slc_prompt), (KV_WIN, new_win_prompt)):
                    sp.dma_start(out[0, 0].rearrange("t c g d -> t (c g d)")[t * P:(t + 1) * P, :],
                                 kvn[:, t, m * P:m * P + ROWW]).then_inc(s_kvout, 16)
            sp.wait_ge(s_kvn, PT_TOK + 1)
            for m, out in ((KV_CMP, new_cmp_sample), (KV_SLC, new_slc_sample)):
                sp.dma_start(out[0].rearrange("b t c g d -> (b t) (c g d)"), kvn[0:TN, PT_TOK, m * P:m * P + ROWW]).then_inc(s_kvout, 16)
            sp.dma_start(new_win_sample[0].rearrange("b t c g d -> b t (c g d)")[:, WIN - TS:WIN, :],
                         kvn[0:TN, PT_TOK, KV_WIN * P:KV_WIN * P + ROWW]).then_inc(s_kvout, 16)

            win_rows = cache_win[0].rearrange("b (p j) c g d -> p b (j c g d)", p=P)
            new_slc = new_slc_sample[0].rearrange("b t c g d -> t b c (g d)")
            new_win = new_win_sample[0].rearrange("b t c g d -> t b c (g d)")
            sp.wait_ge(s_kvout, 16 * (3 * PT_TOK + 3))
            sp.wait_ge(s_pv, 2 + UNITS)
            sp.wait_ge(s_of, 2 * R + 2)

            def load_window(h, i):
                sp.wait_ge(t_pv, 6 * h + 6 + 12 * i)
                sp.dma_start(wb[h][:, :, :].rearrange("p j c -> p (j c)"),
                             win_rows[:, bass.ds(2 * i + h, 1), :].rearrange("p b x -> p (b x)")).then_inc(s_wb[h], 16)
                for m, rows in ((0, new_slc[:, :, 1, :]), (1, new_win[WIN - TS:WIN, :, 1, :])):
                    sp.dma_start(vn[h][:, m, :], rows[:, bass.ds(2 * i + h, 1), :].rearrange("t b x -> t (b x)")).then_inc(s_vn[h], 16)

            with sp.Fori(0, NB // 2) as i:
                for h in range(2):
                    load_window(h, i)

            sp.wait_ge(t_of, 1 + NB)
            sp.dma_start(x_r[:, :, :].rearrange("p k t -> p (k t)"), x_dram).then_inc(s_xr, 16)
            w_att_v = w_out[0][0:CONV, :].rearrange("(a gl r d) n -> a gl d r n", a=2, gl=2, r=R)
            w_cnv_v = w_out[0][CONV:2 * CONV, :].rearrange("(k p) n -> p k n", p=P)

            def out_loads(s, i, u):
                n = bass.ds(i * (2 * P) + u * P, P)
                dst = w_raw[s % 2]
                loads = [(dst[gl * HD:(gl + 1) * HD, 0:CONV].rearrange("p (r a n) -> p r a n", r=R, a=2)[:, :, a, :],
                          w_att_v[a, gl][:, :, n]) for a in range(2) for gl in range(2)]
                return loads + [(dst[:, CONV:2 * CONV].rearrange("p (k n) -> p k n", n=P), w_cnv_v[:, :, n])]

            with sp.Fori(0, KT // 2) as i:
                for u in range(2):
                    load(S_OUT + u, out_loads(S_OUT + u, i, u), it=2 * i)
            w1_v = w_mlp1[0].rearrange("(k p) n -> p k n", p=P)
            w2_v = w_mlp2[0].rearrange("(c k p) n -> p c k n", p=P, k=CT)
            with sp.Fori(0, NCHUNK) as c:
                with sp.Fori(0, CT // 2) as i:
                    for u in range(2):
                        load(S_MLP + u, by_k(S_MLP + u, w1_v[:, :, bass.ds(c * CHUNK + i * (2 * P) + u * P, P)]), it=16 * c + 2 * i)
                with sp.Fori(0, CT // 2) as i:
                    for u in range(2):
                        load(S_MLP + CT + u, by_k(S_MLP + CT + u,
                             w2_v[:, bass.ds(c, 1), :, bass.ds(i * (4 * P) + u * 2 * P, 2 * P)].rearrange("p c k n -> p (c k) n")),
                             it=16 * c + 2 * i)

            for t in range(PT_TOK + 1):
                sp.wait_ge(o_cp, t + 1)
                if t < PT_TOK:
                    sp.dma_start(y_prompt[0, t * P:(t + 1) * P, :], o_rows[t][:, :]).then_inc(s_out, 16)
                else:
                    sp.dma_start(y_sample.rearrange("b t d -> (b t) d"), o_rows[t][0:TN, :]).then_inc(s_out, 16)
            sp.wait_ge(s_out, 16 * (3 + PT_TOK + 1))

        @block.gpsimd
        def _(pool):
            pc = Chain(pool, s_pool)
            pc(nc.gpsimd.memset(ident[:, :], 0.0))
            pc(nc.gpsimd.memset(means[:, :], 1.0 / D))
            pc(nc.gpsimd.memset(sel8[:, :], 1.0))
            pc(nc.gpsimd.memset(spread[:, :], 1.0))
            pc.wait()
            pc(nc.gpsimd.affine_select(out=ident[:, :], in_=ident[:, :], compare_op=ALU.not_equal, fill=1.0,
                                       base=0, pattern=[[-1, P]], channel_multiplier=1))
            pc(nc.gpsimd.affine_select(out=sel8[:, :], in_=sel8[:, :], compare_op=ALU.is_ge, fill=0.0,
                                       base=0, pattern=[[-GROW, P // GROW]], channel_multiplier=1))
            pc(nc.gpsimd.affine_select(out=spread[:, :], in_=spread[:, :], compare_op=ALU.is_ge, fill=0.0,
                                       base=0, pattern=[[1, P]], channel_multiplier=-16))
            pc.wait()
            pc(nc.gpsimd.affine_select(out=sel8[:, :], in_=sel8[:, :], compare_op=ALU.is_ge, fill=0.0,
                                       base=GROW - 1, pattern=[[GROW, P // GROW]], channel_multiplier=-1))
            pc(nc.gpsimd.affine_select(out=spread[:, :], in_=spread[:, :], compare_op=ALU.is_ge, fill=0.0,
                                       base=15, pattern=[[-1, P]], channel_multiplier=16))
            pc(nc.gpsimd.iota(p_of[:, :], pattern=[[0, 1]], base=0, channel_multiplier=1,
                              allow_small_or_imprecise_dtypes=True))
            pc(nc.gpsimd.iota(w_of[:, :], pattern=[[0, 1]], base=0, channel_multiplier=1,
                              allow_small_or_imprecise_dtypes=True))
            pc.wait()
            pool.sem_inc(s_const, 1)

            pool.wait_ge(s_tr, KT)
            pool.wait_ge(s_idx, 1)
            with pool.Fori(0, NGATH // 2) as i:
                for v in range(2):
                    pool.wait_ge(s_gfree, 1 + v + 2 * i)
                    nc.gpsimd.tensor_copy(idx1[v][:, :], idx[:, bass.ds(2 * i + v, 1)]).then_inc(s_idx1, 1)
                    pool.wait_ge(s_idx1, 1 + v + 2 * i)
                    pool.sem_inc(s_asked, 1)
                    nc.gpsimd.indirect_dma_start(
                        gath[v][:, :, :].rearrange("p j c -> p (j c)"), None, cmp_rows,
                        bass.IndirectOffsetOnAxis(ap=idx1[v][:, 0:1], axis=0)).then_inc(s_gath[v], 16)

            pool.wait_ge(s_gemm, 2 + S_OUT)
            pc(nc.gpsimd.memset(qbd[:, :, :, :], 0.0))
            pc(nc.gpsimd.memset(kbd[:, :, :], 0.0))
            pc(nc.gpsimd.memset(causal[:, :], 0.0))
            pc(nc.gpsimd.memset(wmask[:, :], 0.0))
            pc(nc.gpsimd.memset(tri[:, :, :], 1.0))
            pc(nc.gpsimd.memset(gexp[:, :, :], 0.0))
            pc(nc.gpsimd.memset(cbias[:, :, :], 0.0))
            pc.wait()
            pc(nc.gpsimd.affine_select(out=causal[:, :], in_=causal[:, :], compare_op=ALU.is_ge, fill=NEG,
                                       base=TP - P, pattern=[[-1, 2 * TP - P]], channel_multiplier=1))
            pc(nc.gpsimd.affine_select(out=cbias[:, :, :], in_=cbias[:, :, :], compare_op=ALU.is_ge, fill=NEG,
                                       base=1 - BLK, pattern=[[P, PT_TOK], [-BLK, PBLK]], channel_multiplier=1))
            pc(nc.gpsimd.affine_select(out=tri[:, :, :], in_=tri[:, :, :], compare_op=ALU.is_ge, fill=0.0,
                                       base=0, pattern=[[-TS, P // TS], [0, TS]], channel_multiplier=1))
            for br in range(3):
                pc(nc.gpsimd.affine_select(out=gexp[:, br, :].rearrange("c (h t) -> c h t", t=TS),
                                           in_=gexp[:, br, :].rearrange("c (h t) -> c h t", t=TS),
                                           compare_op=ALU.not_equal, fill=1.0, base=-br,
                                           pattern=[[-3, G * R], [0, TS]], channel_multiplier=1))
            pc.wait()
            pc(nc.gpsimd.affine_select(out=tri[:, :, :], in_=tri[:, :, :], compare_op=ALU.is_ge, fill=0.0,
                                       base=-1, pattern=[[TS, P // TS], [1, TS]], channel_multiplier=-1))
            pool.wait_ge(s_cmpv, 2 + NB)
            pc(nc.gpsimd.tensor_copy(cmp_t[:, :, :, :].rearrange("p b m n -> p (b m n)"),
                                     cmp_t0[:, :, :, :].rearrange("p b m n -> p (b m n)")))
            pc.wait()
            pool.sem_inc(s_mask, 1)

            pool.wait_ge(s_pv, 2 + UNITS)
            pool.wait_ge(s_of, 2 + 2 * R)
            with pool.Fori(0, NB // 2) as i:
                for h in range(2):
                    pool.wait_ge(t_qk, 6 * h + 6 + 12 * i)
                    nc.gpsimd.tensor_copy(sq_[h][:, :, :], qbd[:, bass.ds(2 * i + h, 1), :, :].rearrange("p b a n -> p (b a) n")).then_inc(t_qb, 1)
                    for hh in range(2):
                        pool.wait_ge(t_pv, 6 * h + 6 + 12 * i)
                        nc.gpsimd.tensor_copy(idx1[2 * h + hh][:, :], idx[:, bass.ds(4 * i + 2 * h + hh, 1)]).then_inc(t_i, 1)
                        pool.wait_ge(t_i, 2 * h + hh + 1 + 4 * i)
                        pool.sem_inc(s_asked, 1)
                        nc.gpsimd.indirect_dma_start(
                            sg[2 * h + hh][:, :, :].rearrange("p j c -> p (j c)"), None, slc_rows,
                            bass.IndirectOffsetOnAxis(ap=idx1[2 * h + hh][:, 0:1], axis=0)).then_inc(s_sg[2 * h + hh], 16)

        def split_hi(act, s, pairs=0):
            act.wait_ge(s_w[s % 2], raw_in(s, pairs))
            act.wait_ge(s_gemm, s + 1 + 2 * pairs)
            nc.scalar.activation(w_hi[s % 2][:, :], w_raw[s % 2][:, :], ACT.Copy).then_inc(s_hi, 1)

        def split_lo(dve, s, pairs=0):
            dve.wait_ge(s_hi, s + 1 + 2 * pairs)
            nc.vector.tensor_tensor(w_lo[s % 2][:, :], w_raw[s % 2][:, :], w_hi[s % 2][:, :].bitcast(F32),
                                    ALU.subtract).then_inc(s_lo, 1)

        def acc(s):
            return banks(2 * (s % 2), 2, TH)

        @block.scalar
        def _(act):
            split_hi(act, S_GATE)
            split_hi(act, S_CONV)
            with act.Fori(0, KT // 2) as i:
                for v in range(2):
                    act.wait_ge(s_tr, 1 + v + 2 * i)
                    nc.scalar.activation(x_t[:, bass.ds(2 * i + v, 1), :].rearrange("p k t -> p (k t)"), flat(2 * v, T), ACT.Copy).then_inc(s_xt, 1)
                    act.wait_ge(s_xt, 1 + v + 2 * i)
                    nc.scalar.activation(x_hi[:, bass.ds(2 * i + v, 1), :], x_t[:, bass.ds(2 * i + v, 1), :], ACT.Copy).then_inc(s_xhi, 1)
            act.wait_ge(s_gate, 1)
            nc.scalar.activation(gates0[0:NG, :], gates0[0:NG, :], ACT.Sigmoid).then_inc(s_gate, 1)
            with act.Fori(0, (S_OUT - 2) // 2) as i:
                for u in range(2):
                    split_hi(act, 2 + u, i)
            split_hi(act, S_OUT - 1)

            for t in range(PT_TOK + 1):
                n = P if t < PT_TOK else TN
                act.wait_ge(s_kvT, t + 1)
                nc.scalar.activation(kvn[0:n, t, :].rearrange("p (b c) -> p b c", b=3), ps[0:n, 3 * (t % 2):3 * (t % 2) + 3, :], ACT.Copy).then_inc(s_kvn, 1)
            act.wait_ge(s_b, 3)
            nc.scalar.activation(sc[:, :, :], sc[:, :, :], ACT.Exp, scale=SCALE).then_inc(s_a, 1)
            act.wait_ge(s_b, 4)
            nc.scalar.activation(ss[:, :, :], ss[:, :, :], ACT.Exp).then_inc(s_a, 1)
            act.wait_ge(s_one, 7)
            nc.scalar.activation(pct[:, :], ps[:, 0, :], ACT.Copy).then_inc(s_a, 1)
            act.wait_ge(s_one, 9)
            nc.scalar.activation(pcts[:, :, :].rearrange("p b n -> p (b n)"), flat(5, NB * P, NBLK), ACT.Copy).then_inc(s_a, 1)
            act.wait_ge(s_one, 10)
            nc.scalar.activation(vcs[:, :, :, :].rearrange("p (c b) a n -> p c (b a n)", c=4), ps[0:NBLK, 0:4, :], ACT.Copy).then_inc(s_a, 1)
            act.wait_ge(s_out, 48)
            for j in range(2 * R):
                act.wait_ge(s_one, 11 + j)
                nc.scalar.activation(mix[:, j, 0:TP], ps[:, j % 4, :], ACT.Copy).then_inc(s_a, 1)

            def p_exp(u, r):
                act.wait_ge(s_mx, u + 3 + 16 * r)
                i, st, n = (u % 8) // 2, pst[u % 4], ((u % 8) // 2 + 1) * P
                for br in range(2):
                    last = nc.scalar.activation(pS[u % 4][:, br, 0:n], pS[u % 4][:, br, 0:n], ACT.Exp,
                                                bias=st[:, 0, br:br + 1], accum_out=st[:, 1, br:br + 1])
                last.then_inc(s_ex, 1)

            act.sem_inc(s_pe, 1)
            with act.Fori(0, R) as r:
                for a in range(2):
                    act.wait_ge(s_qk, 1 + 16 * r)
                    nc.scalar.activation(pq[a][:, :], q_t[:, bass.ds(r, 1), a, 0:TP].rearrange("p r t -> p (r t)"), ACT.Copy, scale=SCALE).then_inc(s_q, 1)
                p_exp(0, r)
                p_exp(1, r)
                for u in range(16):
                    nk = (u % 8) // 2 + 1
                    act.wait_ge(s_pt_, u + 5 + 16 * r)
                    act.wait_ge(s_pv, u + 1 + 16 * r)
                    nc.scalar.activation(pT[u % 2][:, 0:2 * nk, :].rearrange("p x q -> p (x q)"), flat(4, 2 * nk * P), ACT.Copy).then_inc(s_pe, 1)
                    if u + 2 < 16:
                        p_exp(u + 2, r)

            def k_copy(h, i, c):
                act.wait_ge(t_kt, 5 * h + c + 1 + 10 * i)
                act.wait_ge(t_qk, 6 * h + (10, 11, 13, 14, 15)[c] + 12 * i)
                kp = (h + c) % 2
                nc.scalar.activation(kT[kp][:, :, :], banks(2 * kp, 2, 512), ACT.Copy).then_inc(t_ke, 1)

            def s_exp(h, i):
                act.wait_ge(t_mx, h + 1 + 2 * i)
                for br, (c0, c1) in enumerate(((0, PAST + TS), (PAST + TS, NS_COLS))):
                    last = nc.scalar.activation(sS[h][:, c0:c1], sS[h][:, c0:c1], ACT.Exp,
                                                bias=sst[h][:, 0, br:br + 1], accum_out=sst[h][:, 1, br:br + 1])
                last.then_inc(t_ex, 1)

            def p_copy(h, i, g):
                act.wait_ge(t_pt, 12 + 6 * h + g + 1 + 12 * i)
                act.wait_ge(t_pv, 6 * h + g + 7 + 12 * i)
                bank = 5 + 2 * (g % 2)
                if g < 5:
                    nc.scalar.activation(sT[:, 4 * g:4 * g + 4, :].rearrange("p x q -> p (x q)"), ps[:, bank, :], ACT.Copy).then_inc(t_pe, 1)
                else:
                    nc.scalar.activation(sT[0:TS, 20:22, :].rearrange("p x q -> p (x q)"), ps[0:TS, bank, 0:2 * P], ACT.Copy).then_inc(t_pe, 1)

            def act_phase(k, p):
                for c in range(5):
                    if k:
                        k_copy(*k, c)
                    if p and c == 1:
                        s_exp(*p)
                    if p and c == 3:
                        p_copy(*p, 0)
                for g in range(1, 6):
                    if p:
                        p_copy(*p, g)

            act.sem_inc(t_ke, 2)
            act.sem_inc(t_pe, 2)
            act.wait_ge(s_pv, 2 + UNITS)
            act_phase((0, 0), None)
            with act.Fori(0, NB // 2 - 1) as i:
                act_phase((1, i), (0, i))
                act_phase((0, i + 1), (1, i))
            act_phase((1, NB // 2 - 1), (0, NB // 2 - 1))
            act_phase(None, (1, NB // 2 - 1))

            act.wait_ge(t_of, 1 + NB)
            with act.Fori(0, KT // 2) as i:
                for v in range(2):
                    k = bass.ds(2 * i + v, 1)
                    nc.scalar.activation(mix_hi[:, k, :], mix[:, k, :], ACT.Copy).then_inc(s_mhi, 1)
            split_hi(act, S_OUT)
            split_hi(act, S_OUT + 1)
            with act.Fori(0, KT // 2 - 1) as i:
                for u in range(2):
                    split_hi(act, S_OUT + 2 + u, i)
            split_hi(act, S_MLP)
            split_hi(act, S_MLP + 1)

            def norm_act(turn, g0, b0, split):
                with act.Fori(0, KT // 2) as i:
                    for v in range(2):
                        act.wait_ge(l_sub, KT * turn + v + 1 + 2 * i)
                        act.wait_ge(l_acc, KT * turn + v + 1 + 2 * i)
                        nc.scalar.activation(sqr[v][:, :], h_t[:, bass.ds(2 * i + v, 1), :].rearrange("p k t -> p (k t)"), ACT.Square).then_inc(l_sq, 1)
                act.wait_ge(l_eps, 2 * turn + 1)
                nc.scalar.activation(rstd[:, :], rstd[:, :], ACT.Sqrt).then_inc(l_sd, 1)
                with act.Fori(0, KT // 2) as i:
                    for v in range(2):
                        k = bass.ds(2 * i + v, 1)
                        act.wait_ge(l_mul, KT * turn + v + 1 + 2 * i)
                        nc.scalar.activation(h_t[:, k, :], h_t[:, k, :], ACT.Identity, scale=pars_t[:, bass.ds(g0 + 2 * i + v, 1)],
                                             bias=pars_t[:, bass.ds(b0 + 2 * i + v, 1)]).then_inc(l_aff, 1)
                        if split:
                            act.wait_ge(l_aff, v + 1 + 2 * i)
                            nc.scalar.activation(h_hi[:, k, :], h_t[:, k, :], ACT.Copy).then_inc(l_hi, 1)

            norm_act(0, LN1G, LN1B, True)

            def hidden_act(s, v, c, i):
                act.wait_ge(s_gemm, s + 3 + 16 * c + 2 * i)
                act.wait_ge(f_f, v + 1 + 8 * c + 2 * i)
                nc.scalar.activation(rl[v][:, :].rearrange("p (h t) -> p h t", h=2), acc(s), ACT.Relu).then_inc(f_rl, 1)
                act.wait_ge(f_f, 2 + v + 1 + 8 * c + 2 * i)
                nc.scalar.activation(f_hi[:, bass.ds(2 * i + v, 1), :], fs[v][:, :], ACT.Copy).then_inc(f_h, 1)

            def chunk_act(c, last):
                with act.Fori(0, CT // 2) as i:
                    for u in range(2):
                        hidden_act(S_MLP + u, u, c, i)
                        split_hi(act, S_MLP + u + 2, 8 * c + i)
                with act.Fori(0, CT // 2 - last) as i:
                    for u in range(2):
                        split_hi(act, S_MLP + CT + u + 2, 8 * c + i)

            with act.Fori(0, NCHUNK - 1) as c:
                chunk_act(c, 0)
            chunk_act(NCHUNK - 1, 1)

            norm_act(1, LN2G, LN2B, False)
            for t in range(1, PT_TOK + 1, 2):
                act.wait_ge(o_tr, t + 1)
                act.wait_ge(o_cp, t)
                nc.scalar.activation(o_rows[t][:, :].rearrange("p (b c) -> p b c", b=4), ps[:, 4:8, :], ACT.Copy).then_inc(o_cp, 1)

        @block.vector
        def _(dve):
            dc = Chain(dve, s_dve)
            dve.sem_inc(s_acc, 2)
            dve.sem_inc(s_gfree, 2)
            dve.sem_inc(s_cmpv, 2)
            dve.wait_ge(s_par, 7 * 16)
            dve.wait_ge(s_const, 1)
            dc(nc.vector.tensor_copy(pt_f[:, :], pt_i[:, :]))
            dc.wait()
            nc.vector.tensor_scalar(pt_f[:, :], pt_f[:, :], w_of[:, 0:1], None, ALU.subtract).then_inc(s_pt, 1)
            dve.wait_ge(s_pre, 1)
            nc.vector.tensor_scalar(idx[:, :], ps[:, 4, 0:NGATH], 16.0, p_of[:, 0:1], ALU.mult, ALU.add).then_inc(s_idx, 1)
            dve.wait_ge(s_pre, 2)
            dc(nc.vector.tensor_copy(pars_t[:, :], ps[:, 5, 0:88]))
            dc(nc.vector.tensor_copy(st_t[:, :, :, :].rearrange("p c b j -> p (c b j)"), ps[:, 6, 0:P]))
            dc(nc.vector.tensor_copy(wt[:, :, :].rearrange("p m l -> p (m l)"), ps[:, 7, 0:2 * BLK]))
            split_lo(dve, S_GATE)
            split_lo(dve, S_CONV)
            with dve.Fori(0, KT // 2) as i:
                for v in range(2):
                    dve.wait_ge(s_xhi, 1 + v + 2 * i)
                    k = bass.ds(2 * i + v, 1)
                    nc.vector.tensor_tensor(x_lo[:, k, :], x_t[:, k, :], x_hi[:, k, :].bitcast(F32), ALU.subtract).then_inc(s_xlo, 1)

            def pieces(s):
                a = acc(s)
                return [(a[:, 0, :], 0), (a[:, 1, 0:TP - TH], TH), (a[:, 1, TP - TH:TH], TP)]

            def done(s, it=0):
                dve.wait_ge(s_gemm, s + 3 + it)

            dve.wait_ge(s_xsave, 16)
            dve.wait_ge(s_xlo, KT)
            dc(nc.vector.memset(zpad[:, 0:2], 0.0))
            done(S_GATE)
            nc.vector.tensor_copy(gates0[0:NG, :].rearrange("p (h t) -> p h t", h=2), acc(S_GATE)[0:NG, :, :]).then_inc(s_gate, 1)
            dve.wait_ge(s_gate, 1)
            dve.sem_inc(s_acc, 1)

            def sample(ap, lo, n):
                return ap[:, 2 + TP:2 + TP + NB * (2 + TS)].rearrange("p (b t) -> p b t", b=NB)[:, :, lo:lo + n]

            def fir_sample():
                return fir[:, 2 + TP:2 + TP + NB * (2 + TS)].rearrange("p (b t) -> p b t", b=NB)[:, :, 0:TS]

            def conv_xin(s, it):
                done(s, it)
                dc(nc.vector.tensor_copy(xin[:, :].rearrange("p (h t) -> p h t", h=2), acc(s)))
                dc.wait()
                dve.sem_inc(s_acc, 1)

            def conv_z(s, it, c):
                done(s, it)
                for src, t0 in pieces(s):
                    if t0 < TP:
                        dc(nc.vector.tensor_tensor(zpad[:, 2 + t0:2 + t0 + src.shape[1]], src, xin[:, t0:t0 + src.shape[1]], ALU.mult))
                    else:
                        dc(nc.vector.tensor_tensor(sample(zpad, 2, TS), src.rearrange("p (b t) -> p b t", b=NB),
                                                   xin[:, TP:T].rearrange("p (b t) -> p b t", b=NB), ALU.mult))
                dc(nc.vector.tensor_copy(sample(zpad, 0, 2), st_t[:, bass.ds(c, 1), :, :].rearrange("p c b j -> p (c b) j")))
                dc.wait()
                dve.sem_inc(s_acc, 1)
                dc(nc.vector.tensor_copy(zlast[:, bass.ds(c, 1), 0:2].rearrange("p c j -> p (c j)"), zpad[:, TP:TP + 2]))
                dc(nc.vector.tensor_copy(zlast[:, bass.ds(c, 1), 2:2 + 2 * NB].rearrange("p c (b j) -> p (c b) j", b=NB), sample(zpad, TS, 2)))
                taps = [pars_t[:, bass.ds(CW + j * NCONV + c, 1)] for j in range(3)]
                dc(nc.vector.tensor_scalar(fir[:, 0:ZW - 2], zpad[:, 2:ZW], taps[2], None, ALU.mult))
                for j in range(2):
                    dc.wait()
                    dc(nc.vector.scalar_tensor_tensor(fir[:, 0:ZW - 2], zpad[:, j:j + ZW - 2], taps[j], fir[:, 0:ZW - 2], ALU.mult, ALU.add))

            def conv_y(s, it, c):
                done(s, it)
                dc.wait()
                out = mix[:, bass.ds(NCONV + c, 1), :].rearrange("p c t -> p (c t)")
                for src, t0 in pieces(s):
                    if t0 < TP:
                        dc(nc.vector.tensor_tensor(out[:, t0:t0 + src.shape[1]], src, fir[:, t0:t0 + src.shape[1]], ALU.mult))
                    else:
                        dc(nc.vector.tensor_tensor(out[:, TP:T].rearrange("p (b t) -> p b t", b=NB),
                                                   src.rearrange("p (b t) -> p b t", b=NB), fir_sample(), ALU.mult))
                dc.wait()
                dve.sem_inc(s_acc, 1)

            def compress(i, v):
                g = gath[v % 2]
                dve.wait_ge(s_gath[v % 2], 16 * (v // 2 + 1) + 32 * i)
                for m in range(2):
                    rows = g[:, :, m * G * HD:(m + 1) * G * HD].rearrange("p j (g d) -> p j g d", g=G)
                    wb = wcmp[:, m, :, :].unsqueeze(2).broadcast_to([P, GROW, G, HD])
                    dc(nc.vector.tensor_tensor(rows, rows, wb, ALU.mult))
                dc.wait()
                dve.wait_ge(s_sel, v + 1 + 4 * i)
                nc.vector.tensor_reduce(part[v % 2][:, :], g[:, :, :].rearrange("p j c -> p c j"), AX.X, ALU.add).then_inc(s_part, 1)
                dve.wait_ge(s_part, v + 1 + 4 * i)
                dve.sem_inc(s_gfree, 1)

            def keep_cmp(i, h):
                dve.wait_ge(s_sel, 2 + 2 * h + 2 + 4 * i)
                nc.vector.tensor_copy(cmp_t0[:, bass.ds(2 * i + h, 1), :, :].rearrange("p b m n -> p (b m n)"),
                                      ps[:, 4 + h, 0:4 * NBLK]).then_inc(s_cmpv, 1)

            dve.wait_ge(s_wcmp, 32)
            split_lo(dve, S_CONV + 1)
            for i in dc.turns(NCONV // 2, 34):
                for u in range(6):
                    s, c = S_CONV + u, 2 * i + u // 3
                    if u % 3 == 0:
                        conv_xin(s, 6 * i)
                    elif u % 3 == 1:
                        conv_z(s, 6 * i, c)
                    else:
                        conv_y(s, 6 * i, c)
                    split_lo(dve, s + 2, 3 * i)
                    if u in (0, 1, 3, 4):
                        compress(i, (0, 1, None, 2, 3)[u])
                    if u == 3:
                        keep_cmp(i, 0)
                    if u == 5:
                        keep_cmp(i, 1)

            def keep(dst, s, it):
                done(s, it)
                nc.vector.tensor_copy(dst.rearrange("p (h t) -> p h t", h=2), acc(s)).then_inc(s_acc, 1)

            with dve.Fori(0, R) as r:
                for a in range(2):
                    keep(q_t[:, bass.ds(r, 1), a, :].rearrange("p r t -> p (r t)"), S_Q + a, 2 * r)
                    split_lo(dve, S_Q + a + 2, r)
            with dve.Fori(0, NKV // 2 - 1) as i:
                for u in range(2):
                    keep(kv_t[:, bass.ds(2 * i + u, 1), :].rearrange("p r t -> p (r t)"), S_KV + u, 2 * i)
                    split_lo(dve, S_KV + u + 2, i)
            keep(kv_t[:, NKV - 2, :], S_KV + NKV - 2, 0)
            keep(kv_t[:, NKV - 1, :], S_KV + NKV - 1, 0)
            dve.wait_ge(s_zlT, 1)
            nc.vector.tensor_copy(zl_rows[:, :], flat(4, CONV, 2 + 2 * NB)).then_inc(s_zlv, 1)

            dve.wait_ge(s_one, 1)
            dc(nc.vector.tensor_copy(gn[:, :, :].rearrange("p t c -> p (t c)"), ps[:, 6, 0:PT_TOK * NG]))
            for m in range(2):
                rows = kv_t[:, KV_CMP + 2 * m:KV_CMP + 2 * m + 2, 0:TP].rearrange("p a (n l) -> p a n l", l=BLK)
                wb_ = wt[:, m, :].unsqueeze(1).unsqueeze(1).broadcast_to([P, 2, PBLK, BLK])
                dc(nc.vector.tensor_tensor(tmp[m][:, :, :, :], rows, wb_, ALU.mult))
            dc.wait()
            for m in range(2):
                dc(nc.vector.tensor_reduce(kc[:, 2 * m:2 * m + 2, :], tmp[m][:, :, :, :], AX.X, ALU.add))
            dve.wait_ge(s_mask, 1)
            dc(nc.vector.tensor_reduce(tok_of[:, :], ident[:, :].rearrange("p (x t) -> p t x", t=TS), AX.X, ALU.add))
            dc(nc.vector.tensor_reduce(grp_of[:, :], ident[:, :].rearrange("p (g x) -> p g x", g=G), AX.X, ALU.add))
            dc(nc.vector.tensor_reduce(pair_of[:, :], ident[:, :].rearrange("p (j n) -> p j n", n=PBLK), AX.X, ALU.add))
            dc(nc.vector.tensor_reduce(before[:, :], tri[:, :, :].rearrange("p x t -> p t x"), AX.X, ALU.add))
            dc(nc.vector.tensor_copy(e8[:, :].rearrange("n (x m) -> n x m", m=PBLK),
                                     ident[0:PBLK, 0:PBLK].unsqueeze(1).broadcast_to([PBLK, P // PBLK, PBLK])))
            dc.wait()
            for g in range(G):
                dc(nc.vector.tensor_scalar(same[:, g * 32:(g + 1) * 32].rearrange("p (r t) -> p r t", r=R),
                                           tok_of[:, :].unsqueeze(1).broadcast_to([P, R, TS]), grp_of[:, g:g + 1], None, ALU.mult))
            for m in range(2):
                dc(nc.vector.tensor_scalar(nmask[:, m, :], before[:, :], NEG, None, ALU.mult))
            dc(nc.vector.tensor_scalar(wmask[:, :].rearrange("p (j c) -> p j c", j=4)[:, :, 0:2],
                                       before[:, :].rearrange("p (q j) -> p j q", j=4), -NEG, NEG, ALU.mult, ALU.add))
            dve.wait_ge(s_one, 2)
            dc(nc.vector.tensor_tensor(gtmp[:, :, :].rearrange("p m (b t) -> p (m b) t", t=TS),
                                       ps[:, 7, 0:3 * TN].rearrange("p (x t) -> p x t", t=TS),
                                       tok_of[:, :].unsqueeze(1).broadcast_to([P, 3 * NB, TS]), ALU.mult))
            for gl in range(2):
                half = slice(gl * HD, (gl + 1) * HD)
                dc(nc.vector.tensor_copy(kbd[half, :, gl * PBLK:(gl + 1) * PBLK], kc[half, 0:2, :]))
                for a in range(2):
                    g = 2 * a + gl
                    dc(nc.vector.tensor_scalar(qbd[half, :, a, g * 32:(g + 1) * 32].rearrange("p b (r t) -> p b r t", r=R),
                                               q_t[half, :, a, TP:T].rearrange("p r (b t) -> p b r t", b=NB), SCALE, None, ALU.mult))
            for m, kv in enumerate((KV_SLC, KV_WIN)):
                dc(nc.vector.tensor_copy(kn[:, m, :, :], kv_t[:, kv:kv + 2, TP:T]))
            dc.wait()
            dc(nc.vector.tensor_reduce(gs[:, :, :].rearrange("p m b -> p (m b)"),
                                       gtmp[:, :, :].rearrange("p m (b t) -> p (m b) t", t=TS), AX.X, ALU.add))
            dc.wait()
            dve.sem_inc(s_b, 1)
            dve.wait_ge(s_one, 3)
            nc.vector.tensor_copy(vcn[:, :], ps[0:PBLK, 0, 0:G * HD]).then_inc(s_b, 1)
            dve.wait_ge(s_one, 4)
            dc(nc.vector.tensor_tensor(sc[:, :, :].rearrange("p i (x n) -> p i x n", n=PBLK),
                                       ps[:, 1, :].rearrange("p (i x n) -> p i x n", i=PT_TOK, n=PBLK),
                                       cbias[:, :, :].unsqueeze(2).broadcast_to([P, PT_TOK, 16, PBLK]), ALU.add))
            dc.wait()
            heads = sc[:, :, :].rearrange("p i (x n) -> p (i x) n", n=PBLK)
            dc(nc.vector.tensor_reduce(st1[:, :], heads, AX.X, ALU.max))
            dc.wait()
            dc(nc.vector.tensor_scalar(st1[:, :], st1[:, :], NEG / 10, None, ALU.max))
            dc.wait()
            dve.wait_ge(s_b, 2)
            nc.vector.tensor_tensor(heads, heads, st1[:, :].unsqueeze(2).broadcast_to([P, PT_TOK * 16, PBLK]), ALU.subtract).then_inc(s_b, 1)
            dve.wait_ge(s_one, 5)
            seqs = ps[:, 2, 0:NB * NBLK].rearrange("p (b n) -> p b n", b=NB)
            dc(nc.vector.tensor_reduce(st3[:, :], seqs, AX.X, ALU.max))
            dc.wait()
            dve.wait_ge(s_b, 3)
            nc.vector.tensor_tensor(ss[:, :, :], seqs, st3[:, :].unsqueeze(2).broadcast_to([P, NB, NBLK]), ALU.subtract).then_inc(s_b, 1)
            dve.wait_ge(s_one, 6)
            for a in range(2):
                last = nc.vector.tensor_tensor(
                    vbd[:, a:2 * R:2, :].rearrange("p r (g d) -> p r g d", g=2),
                    ps[:, 3, a * P:(a + 1) * P].rearrange("p (g d) -> p g d", g=2).unsqueeze(1).broadcast_to([P, R, 2, HD]),
                    pair_of[:, :].rearrange("p (r a g) -> p a r g", a=2, g=2)[:, a].unsqueeze(3).broadcast_to([P, R, 2, HD]), ALU.mult)
            last.then_inc(s_b, 1)
            dve.wait_ge(s_a, 1)
            dc(nc.vector.tensor_reduce(st2[:, :], heads, AX.X, ALU.add))
            dc.wait()
            dc(nc.vector.tensor_scalar(st2[:, :], st2[:, :], 1e-30, None, ALU.max))
            dc.wait()
            dc(nc.vector.reciprocal(st2[:, :], st2[:, :]))
            dc.wait()
            for i in range(PT_TOK):
                dc(nc.vector.tensor_tensor(st1[:, i * 16:(i + 1) * 16].rearrange("p (r a g) -> p r a g", r=R, a=2),
                                           st2[:, i * 16:(i + 1) * 16].rearrange("p (r a g) -> p r a g", r=R, a=2),
                                           gn[:, i, :].rearrange("p (a g r m) -> p m r a g", a=2, g=2, r=R)[:, 0], ALU.mult))
            dc.wait()
            nc.vector.tensor_tensor(heads, heads, st1[:, :].unsqueeze(2).broadcast_to([P, PT_TOK * 16, PBLK]), ALU.mult).then_inc(s_b, 1)
            dve.wait_ge(s_a, 2)
            dc(nc.vector.tensor_reduce(st4[:, :], ss[:, :, :], AX.X, ALU.add))
            dc.wait()
            dc(nc.vector.reciprocal(st4[:, :], st4[:, :]))
            dc.wait()
            nc.vector.tensor_tensor(ss[:, :, :], ss[:, :, :], st4[:, :].unsqueeze(2).broadcast_to([P, NB, NBLK]), ALU.mult).then_inc(s_b, 1)
            dve.wait_ge(s_b, 7)
            nc.vector.tensor_tensor(pg[:, :, :], ss[:, :, :], gs[:, 0, :].unsqueeze(2).broadcast_to([P, NB, NBLK]), ALU.mult).then_inc(s_b, 1)
            dc(nc.vector.memset(vals[:, :, :], -1.0))
            dve.wait_ge(s_one, 8)
            dc.wait()
            dc(nc.vector.tensor_copy(vals[:, :, 1:NBLK - 1], ps[:, 4, 0:NB * NBLK].rearrange("p (b n) -> p b n", b=NB)[:, :, 1:NBLK - 1]))
            dc.wait()
            for b in range(NB):
                row = vals[:, b, :]
                dc(nc.vector.max(m8[:, :], row))
                dc.wait()
                dc(nc.vector.match_replace(row, m8[:, :], row, -2.0))
                dc.wait()
                dc(nc.vector.max(m5[:, :], row))
                dc.wait()
                dc(nc.vector.memset(m5[:, NSEL - FORCED - 8:8], -1.0))
                dc.wait()
                dc(nc.vector.match_replace(row, m5[:, :], row, -2.0))
                dc.wait()
            dc(nc.vector.tensor_scalar(mb[:, :, :], vals[:, :, 0:NBLK], -1.5, NEG, ALU.is_gt, ALU.mult))
            dc.wait()
            dc(nc.vector.memset(mb[:, :, 0:1], 0.0))
            dc(nc.vector.memset(mb[:, :, NBLK - 1:NBLK], 0.0))
            dc.wait()
            dve.sem_inc(s_b, 1)
            dve.wait_ge(s_one, 19)
            outs = flat(4, NB * P).rearrange("p (b a g x) -> p b a g x", b=NB, a=2, g=2)
            for gl in range(2):
                for a in range(2):
                    half = slice(gl * HD, (gl + 1) * HD)
                    dc(nc.vector.tensor_copy(mix[half, a:2 * R:2, TP:T].rearrange("p r (b t) -> p b r t", b=NB),
                                             outs[half, :, a, gl, :].rearrange("p b (r t) -> p b r t", r=R)))
            dve.wait_ge(s_a, 5 + 2 * R)
            dc.wait()
            dve.sem_inc(s_b, 1)

            def p_scores(u, r):
                i, st, n = (u % 8) // 2, pst[u % 4], ((u % 8) // 2 + 1) * P
                b0 = 2 * (u % 2)
                dve.wait_ge(s_qk, u + 2 + 16 * r)
                dve.wait_ge(s_pt_, u + 1 + 16 * r)
                dc(nc.vector.tensor_tensor(pS[u % 4][:, :, 0:n], banks(b0, 2, n),
                                           causal[:, TP - n:TP].unsqueeze(1).broadcast_to([P, 2, n]), ALU.add))
                dc.wait()
                nc.vector.tensor_reduce(st[:, 0, :], pS[u % 4][:, :, 0:n], AX.X, ALU.max, negate=True).then_inc(s_mx, 1)

            def p_scale(u, r):
                i, st, n = (u % 8) // 2, pst[u % 4], ((u % 8) // 2 + 1) * P
                g = 2 * (u // 8) + u % 2
                dve.wait_ge(s_ex, u + 1 + 16 * r)
                dc(nc.vector.reciprocal(st[:, 2, :], st[:, 1, :]))
                dc.wait()
                dc(nc.vector.tensor_tensor(st[:, 2, :], st[:, 2, :], gn[:, i, bass.ds(g * 12 + r * 3 + 1, 2)], ALU.mult))
                dc.wait()
                for br in range(2):
                    last = nc.vector.tensor_scalar(pS[u % 4][:, br, 0:n], pS[u % 4][:, br, 0:n], st[:, 2, br:br + 1], None, ALU.mult)
                last.then_inc(s_sc, 1)

            def p_out(a, r):
                dve.wait_ge(s_pv, 8 * a + 7 + 3 + 16 * r)
                tile = mix[:, bass.ds(2 * r + a, 1), 0:TP].rearrange("p j t -> p (j t)")
                nc.vector.tensor_tensor(tile, tile, ps[:, 6 + a, :], ALU.add).then_inc(s_of, 1)

            dve.sem_inc(s_mx, 2)
            dve.sem_inc(s_of, 2)
            for r in dc.turns(R, 48):
                p_scores(0, r)
                p_scores(1, r)
                for u in range(16):
                    p_scale(u, r)
                    if u + 2 < 16:
                        p_scores(u + 2, r)
                    if u == 10:
                        p_out(0, r)
                p_out(1, r)

            def k_scores(h, i, c):
                dve.wait_ge(t_qk, 12 + 6 * h + c + 1 + 12 * i)
                if c == 0:
                    dve.wait_ge(t_pt, 6 * h + 6 + 12 * i)
                if c < 4:
                    hh = c // 2
                    bias = mb[:, bass.ds(2 * i + h, 1), hh * 16:(hh + 1) * 16].rearrange("p b n -> p (b n)")
                    ins = nc.vector.tensor_tensor(sS[h][:, c * 512:(c + 1) * 512].rearrange("p (j n s) -> p j n s", j=4, s=GROW),
                                                  ps[:, 4, :].rearrange("p (j n s) -> p j n s", j=4, s=GROW),
                                                  bias.unsqueeze(1).unsqueeze(3).broadcast_to([P, 4, 16, GROW]), ALU.add)
                elif c == 4:
                    ins = nc.vector.tensor_tensor(sS[h][:, PAST + TS:PAST + TS + WIN], ps[:, 4, :], wmask[:, :], ALU.add)
                else:
                    for m, at_ in enumerate((PAST, PAST + TS + WIN)):
                        ins = nc.vector.tensor_tensor(sS[h][:, at_:at_ + TS], ps[:, 4, m * TS:(m + 1) * TS], nmask[:, m, :], ALU.add)
                ins.then_inc(t_se, 1)

            def k_max(h, i):
                dve.wait_ge(t_se, 1 + 6 * h + 6 + 12 * i)
                for br, (c0, c1) in enumerate(((0, PAST + TS), (PAST + TS, NS_COLS))):
                    last = nc.vector.tensor_reduce(sst[h][:, 0, br:br + 1], sS[h][:, c0:c1], AX.X, ALU.max, negate=True)
                last.then_inc(t_mx, 1)

            def s_scale(h, i):
                st = sst[h]
                dve.wait_ge(t_ex, h + 1 + 2 * i)
                dc(nc.vector.reciprocal(st[:, 2, :], st[:, 1, :]))
                dc.wait()
                dc(nc.vector.tensor_tensor(st[:, 2, :], st[:, 2, :], gs[:, 1:3, bass.ds(2 * i + h, 1)].rearrange("p m b -> p (m b)"), ALU.mult))
                dc.wait()
                for br, (c0, c1) in enumerate(((0, PAST + TS), (PAST + TS, NS_COLS))):
                    last = nc.vector.tensor_scalar(sS[h][:, c0:c1], sS[h][:, c0:c1], st[:, 2, br:br + 1], None, ALU.mult)
                last.then_inc(t_sc, 1)

            def s_out_add(h, i):
                dve.wait_ge(t_pv, 12 + 6 * h + 6 + 12 * i)
                for gl in range(2):
                    half = slice(gl * HD, (gl + 1) * HD)
                    tile = mix[half, 0:2 * R, bass.ds(16 * i + TP + TS * h, TS)].rearrange("p (r a) t -> p a r t", a=2)
                    last = nc.vector.tensor_tensor(
                        tile, tile, ps[half, 6, 0:P].rearrange("p (a g r t) -> p g a r t", a=2, g=2, r=R)[:, gl], ALU.add)
                last.then_inc(t_of, 1)

            def dve_phase(k, p):
                for c in range(6):
                    if k:
                        k_scores(*k, c)
                    if p and c == 1:
                        s_scale(*p)
                if k:
                    k_max(*k)
                if p:
                    s_out_add(*p)

            dve.sem_inc(t_se, 1)
            dve.sem_inc(t_of, 1)
            dve.wait_ge(s_kvout, 16 * (3 * PT_TOK + 3))
            dve_phase((0, 0), None)
            for i in dc.turns(NB // 2 - 1, 4):
                dve_phase((1, i), (0, i))
                dve_phase((0, i + 1), (1, i))
            dve_phase((1, NB // 2 - 1), (0, NB // 2 - 1))
            dve_phase(None, (1, NB // 2 - 1))

            with dve.Fori(0, KT // 2) as i:
                for v in range(2):
                    k = bass.ds(2 * i + v, 1)
                    dve.wait_ge(s_mhi, v + 1 + 2 * i)
                    nc.vector.tensor_tensor(mix_lo[:, k, :], mix[:, k, :], mix_hi[:, k, :].bitcast(F32), ALU.subtract).then_inc(s_mlo, 1)
            split_lo(dve, S_OUT)
            split_lo(dve, S_OUT + 1)
            dve.wait_ge(s_xr, 16)

            def residual(s, i, u):
                done(s, 2 * i)
                k = bass.ds(2 * i + u, 1)
                nc.vector.scalar_tensor_tensor(h_t[:, k, :].rearrange("p k (h t) -> p (k h) t", h=2),
                                               x_r[:, k, :].rearrange("p k (h t) -> p (k h) t", h=2), ALPHA,
                                               acc(s), ALU.mult, ALU.add).then_inc(s_acc, 1)

            dve.wait_ge(s_mlo, KT)
            with dve.Fori(0, KT // 2 - 1) as i:
                for u in range(2):
                    residual(S_OUT + u, i, u)
                    split_lo(dve, S_OUT + u + 2, i)
            for u in range(2):
                k = KT - 2 + u
                done(S_OUT + k)
                nc.vector.scalar_tensor_tensor(h_t[:, k, :].rearrange("p (h t) -> p h t", h=2),
                                               x_r[:, k, :].rearrange("p (h t) -> p h t", h=2), ALPHA,
                                               acc(S_OUT + k), ALU.mult, ALU.add).then_inc(s_acc, 1)
            split_lo(dve, S_MLP)
            split_lo(dve, S_MLP + 1)

            def norm_dve(turn, split):
                dve.wait_ge(l_mean, turn + 1)
                with dve.Fori(0, KT // 2) as i:
                    for v in range(2):
                        k = bass.ds(2 * i + v, 1)
                        view = h_t[:, k, :].rearrange("p k (h t) -> p (k h) t", h=2)
                        nc.vector.tensor_tensor(view, view, banks(4, 2, TH), ALU.subtract).then_inc(l_sub, 1)
                dve.wait_ge(l_acc, 2 + KT * (turn + 1))
                nc.vector.tensor_scalar(rstd[:, :].rearrange("p (h t) -> p h t", h=2), banks(6, 2, TH), EPS, None, ALU.add).then_inc(l_eps, 1)
                dve.wait_ge(l_sd, turn + 1)
                nc.vector.reciprocal(rstd[:, :], rstd[:, :]).then_inc(l_eps, 1)
                dve.wait_ge(l_eps, 2 * turn + 2)
                with dve.Fori(0, KT // 2) as i:
                    for v in range(2):
                        k = bass.ds(2 * i + v, 1)
                        view = h_t[:, k, :].rearrange("p k t -> p (k t)")
                        nc.vector.tensor_tensor(view, view, rstd[:, :], ALU.mult).then_inc(l_mul, 1)
                        if split:
                            if v:
                                split_tail(i, 0)
                                split_tail(i, 1)

            def split_tail(i, v):
                k = bass.ds(2 * i + v, 1)
                dve.wait_ge(l_hi, v + 1 + 2 * i)
                nc.vector.tensor_tensor(h_lo[:, k, :], h_t[:, k, :], h_hi[:, k, :].bitcast(F32), ALU.subtract).then_inc(l_lo, 1)
                dve.wait_ge(l_lo, v + 1 + 2 * i)
                nc.vector.tensor_scalar(h_t[:, k, :], h_t[:, k, :], ALPHA, None, ALU.mult).then_inc(l_al, 1)

            norm_dve(0, True)
            dve.wait_ge(l_al, KT)
            dve.sem_inc(f_f, 2)

            def hidden_dve(s, v, c, i):
                dve.wait_ge(f_rl, v + 1 + 8 * c + 2 * i)
                dve.wait_ge(f_l, v + 1 + 8 * c + 2 * i)
                nc.vector.scalar_tensor_tensor(fs[v][:, :].rearrange("p (h t) -> p h t", h=2), acc(s), 0.0,
                                               rl[v][:, :].rearrange("p (h t) -> p h t", h=2), ALU.max, ALU.mult).then_inc(f_f, 1)
                dve.wait_ge(f_f, 2 + v + 1 + 8 * c + 2 * i)
                dve.sem_inc(s_acc, 1)
                dve.wait_ge(f_h, v + 1 + 8 * c + 2 * i)
                nc.vector.tensor_tensor(f_lo[:, bass.ds(2 * i + v, 1), :].rearrange("p k t -> p (k t)"), fs[v][:, :],
                                        f_hi[:, bass.ds(2 * i + v, 1), :].rearrange("p k t -> p (k t)").bitcast(F32), ALU.subtract).then_inc(f_l, 1)

            def add_out(s, c, i, u):
                done(s, 16 * c + 2 * i)
                for j in range(2):
                    view = h_t[:, bass.ds(4 * i + 2 * u + j, 1), :].rearrange("p k (h t) -> p (k h) t", h=2)
                    last = nc.vector.tensor_tensor(view, view, banks(2 * (s % 2) + 4 * j, 2, TH), ALU.add)
                last.then_inc(s_acc, 1)

            def chunk_dve(c, last):
                with dve.Fori(0, CT // 2) as i:
                    for u in range(2):
                        hidden_dve(S_MLP + u, u, c, i)
                        split_lo(dve, S_MLP + u + 2, 8 * c + i)
                with dve.Fori(0, CT // 2 - last) as i:
                    for u in range(2):
                        add_out(S_MLP + CT + u, c, i, u)
                        split_lo(dve, S_MLP + CT + u + 2, 8 * c + i)
                for u in range(2 * last):
                    add_last(c, u)

            def add_last(c, u):
                s = S_MLP + 2 * CT - 2 + u
                done(s, 16 * c)
                for j in range(2):
                    view = h_t[:, KT - 4 + 2 * u + j, :].rearrange("p (h t) -> p h t", h=2)
                    last = nc.vector.tensor_tensor(view, view, banks(2 * (s % 2) + 4 * j, 2, TH), ALU.add)
                last.then_inc(s_acc, 1)

            dve.sem_inc(f_l, 2)
            with dve.Fori(0, NCHUNK - 1) as c:
                chunk_dve(c, 0)
            chunk_dve(NCHUNK - 1, 1)

            norm_dve(1, False)
            for t in range(0, PT_TOK + 1, 2):
                n = P if t < PT_TOK else TN
                dve.wait_ge(o_tr, t + 1)
                if t:
                    dve.wait_ge(o_cp, t)
                nc.vector.tensor_copy(o_rows[t][0:n, :].rearrange("p (b c) -> p b c", b=4), ps[0:n, 0:4, :]).then_inc(o_cp, 1)

        @block.tensor
        def _(pe):
            pe.sem_inc(s_gemm, 2)
            pe.sem_inc(s_sel, 2)
            pe.wait_ge(s_const, 1)
            pe.wait_ge(s_pt, 1)
            pe.wait_ge(s_wr, 64)
            nc.tensor.matmul(ps[:, 4, 0:NGATH], spread[:, :], pt_f[:, :], start=True, stop=True).then_inc(s_pre, 1)
            nc.tensor.transpose(ps[:, 5, 0:88], pars[:, :], ident[0:88, 0:88])
            for c in range(NCONV):
                last = nc.tensor.transpose(ps[:, 6, c * 16:(c + 1) * 16], st_in[:, c * P:(c + 1) * P], ident[0:2 * NB, 0:2 * NB])
            for m in range(2):
                last = nc.tensor.transpose(ps[:, 7, m * BLK:(m + 1) * BLK], w_rows[:, m * P:(m + 1) * P], ident[0:BLK, 0:BLK])
            last.then_inc(s_pre, 1)
            for k in range(KT):
                if k >= 2:
                    pe.wait_ge(s_xt, k - 1)
                for t in range(PT_TOK + 1):
                    n = P if t < PT_TOK else TN
                    if k == 0:
                        pe.wait_ge(s_x[t], 16)
                    last = nc.tensor.transpose(flat(2 * (k % 2), t * P + n)[:, t * P:t * P + n],
                                               x_rows[0:n, t, k * P:(k + 1) * P], ident[0:n, 0:n])
                last.then_inc(s_tr, 1)

            def gemm(s, it, acts, kts=KT, tiles=1, n=P):
                pe.wait_ge(s_lo, s + 1 + it)
                pe.wait_ge(s_acc, s + 1 + it)
                hi, lo = w_hi[s % 2], w_lo[s % 2]
                a_hi, a_lo = acts
                for j in range(tiles):
                    out = banks(2 * (s % 2) + 4 * j, 2, TH)
                    for k in range(kts):
                        at_ = (k * tiles + j) * n
                        for m, (w, x) in enumerate(((hi, a_hi), (hi, a_lo), (lo, a_hi))):
                            for h in range(2):
                                last = nc.tensor.matmul(out[:, h, :], w[:, at_:at_ + n], x[:, k, h * TH:(h + 1) * TH],
                                                        start=(k == 0 and m == 0), stop=(k == kts - 1 and m == 2))
                last.then_inc(s_gemm, 1)

            pe.wait_ge(s_xhi, KT)
            pe.wait_ge(s_xlo, KT)
            x_parts = (x_hi, x_lo)
            gemm(S_GATE, 0, x_parts)

            def sum_blocks(i, v):
                pe.wait_ge(s_part, v + 1 + 4 * i)
                if v % 2 == 0:
                    pe.wait_ge(s_cmpv, v // 2 + 1 + 2 * i)
                for m in range(4):
                    o = m * NBLK + (v % 2) * (NBLK // 2)
                    last = nc.tensor.matmul(ps[:, 4 + v // 2, o:o + NBLK // 2], part[v % 2][:, m * P:(m + 1) * P],
                                            sel8[:, :], start=True, stop=True)
                last.then_inc(s_sel, 1)

            with pe.Fori(0, NCONV // 2) as i:
                for u in range(6):
                    gemm(S_CONV + u, 6 * i, x_parts)
                    if u in (1, 2, 4, 5):
                        sum_blocks(i, (None, 0, 1, None, 2, 3)[u])
            pe.wait_ge(s_cmpv, 2 + NB)
            for c in range(NCONV):
                last = nc.tensor.transpose(flat(4, CONV, 2 + 2 * NB)[:, c * P:(c + 1) * P], zlast[:, c, :], ident[:, :])
            last.then_inc(s_zlT, 1)
            with pe.Fori(0, (8 + NKV) // 2) as i:
                for u in range(2):
                    gemm(S_Q + u, 2 * i, x_parts)

            pe.wait_ge(s_acc, 2 + S_OUT)
            pe.wait_ge(s_zlv, 1)
            for t in range(PT_TOK + 1):
                n = P if t < PT_TOK else TN
                if t >= 2:
                    pe.wait_ge(s_kvn, t - 1)
                for m in range(NKV):
                    last = nc.tensor.transpose(ps[0:n, 3 * (t % 2) + m // 4, (m % 4) * P:(m % 4 + 1) * P],
                                               kv_t[:, m, t * P:t * P + n], ident[:, :])
                last.then_inc(s_kvT, 1)
            pe.wait_ge(s_gate, 2)
            for t in range(PT_TOK):
                last = nc.tensor.transpose(ps[:, 6, t * NG:(t + 1) * NG], gates0[0:NG, t * P:(t + 1) * P], ident[0:NG, 0:NG])
            last.then_inc(s_one, 1)
            pe.wait_ge(s_mask, 1)
            for m in range(3):
                last = nc.tensor.matmul(ps[:, 7, m * TN:(m + 1) * TN], gexp[:, m, :], gates0[0:NG, TP:T], start=True, stop=True)
            last.then_inc(s_one, 1)
            pe.wait_ge(s_b, 1)
            pe.wait_ge(s_kvn, PT_TOK + 1)
            for a in range(2):
                last = nc.tensor.transpose(ps[0:PBLK, 0, a * P:(a + 1) * P], kc[:, 2 + a, :], ident[:, :])
            last.then_inc(s_one, 1)
            for i in range(PT_TOK):
                for r in range(R):
                    for a in range(2):
                        o = i * P + (2 * r + a) * 16
                        last = nc.tensor.matmul(ps[:, 1, o:o + 16], q_t[:, r, a, i * P:(i + 1) * P], kbd[:, a, :], start=True, stop=True)
            last.then_inc(s_one, 1)
            for b in range(NB):
                for a in range(2):
                    last = nc.tensor.matmul(ps[:, 2, b * NBLK:(b + 1) * NBLK], qbd[:, b, a, :], cmp_t[:, b, a, :], start=(a == 0), stop=(a == 1))
            last.then_inc(s_one, 1)
            pe.wait_ge(s_b, 2)
            nc.tensor.matmul(ps[:, 3, 0:G * HD], e8[:, :], vcn[:, :], start=True, stop=True).then_inc(s_one, 1)
            pe.wait_ge(s_b, 6)
            for i in range(PT_TOK):
                last = nc.tensor.transpose(ps[:, 0, i * P:(i + 1) * P], sc[:, i, :], ident[:, :])
            last.then_inc(s_one, 1)
            pe.wait_ge(s_b, 7)
            nc.tensor.matmul(ps[:, 4, 0:NB * NBLK], same[:, :], ss[:, :, :].rearrange("p b n -> p (b n)"), start=True, stop=True).then_inc(s_one, 1)
            pe.wait_ge(s_b, 8)
            for b in range(NB):
                last = nc.tensor.transpose(flat(5, NB * P, NBLK)[:, b * P:(b + 1) * P], pg[:, b, :], ident[:, :])
            last.then_inc(s_one, 1)
            pe.wait_ge(s_a, 3)
            for b in range(NB):
                for a in range(2):
                    m = 2 * b + a
                    last = nc.tensor.transpose(ps[0:NBLK, m // 4, (m % 4) * P:(m % 4 + 1) * P], cmp_t[:, b, 2 + a, :], ident[:, :])
            last.then_inc(s_one, 1)
            for j in range(2 * R):
                pe.wait_ge(s_a, 5 + max(0, j - 3))
                nc.tensor.matmul(ps[:, j % 4, :], vbd[:, j, :], pct[:, :], start=True, stop=True).then_inc(s_one, 1)
            pe.wait_ge(s_b, 9)
            for b in range(NB):
                for a in range(2):
                    o = (2 * b + a) * HD
                    last = nc.tensor.matmul(flat(4, NB * P)[:, o:o + HD], vcs[:, b, a, :], pcts[:, b, a * HD:(a + 1) * HD], start=True, stop=True)
            last.then_inc(s_one, 1)

            def p_qk(u, r):
                a, gl, n = u // 8, u % 2, ((u % 8) // 2 + 1) * P
                half = slice(gl * HD, (gl + 1) * HD)
                if u % 8 == 0:
                    pe.wait_ge(s_q, a + 1 + 2 * r)
                pe.wait_ge(s_mx, u + 1 + 16 * r)
                for br, kv in enumerate((KV_SLC, KV_WIN)):
                    last = nc.tensor.matmul(ps[:, 2 * (u % 2) + br, 0:n], pq[a][half, n - P:n], kv_t[half, kv + a, 0:n], start=True, stop=True)
                last.then_inc(s_qk, 1)

            def p_turn(u, r):
                nk = (u % 8) // 2 + 1
                pe.wait_ge(s_sc, u + 1 + 16 * r)
                pe.wait_ge(s_pe, u + 1 + 16 * r)
                for x in range(2 * nk):
                    br, kt = x // nk, x % nk
                    last = nc.tensor.transpose(ps[:, 4 + x // 4, (x % 4) * P:(x % 4 + 1) * P], pS[u % 4][:, br, kt * P:(kt + 1) * P], ident[:, :])
                last.then_inc(s_pt_, 1)

            def p_pv(u, r):
                a, i, gl = u // 8, (u % 8) // 2, u % 2
                nk = i + 1
                if u % 8 == 0:
                    pe.wait_ge(s_of, a + 1 + 2 * r)
                pe.wait_ge(s_pe, u + 2 + 16 * r)
                for x in range(2 * nk):
                    br, kt = x // nk, x % nk
                    v0 = ((KV_SLC, KV_WIN)[br] + 2 + a) * P + gl * HD
                    last = nc.tensor.matmul(ps[gl * HD:(gl + 1) * HD, 6 + a, i * P:(i + 1) * P], kvn[:, kt, v0:v0 + HD], pT[u % 2][:, x, :],
                                            start=(x == 0), stop=(x == 2 * nk - 1))
                last.then_inc(s_pv, 1)

            pe.wait_ge(s_b, 10)
            pe.sem_inc(s_qk, 1)
            pe.sem_inc(s_pt_, 4)
            pe.sem_inc(s_pv, 2)
            with pe.Fori(0, R) as r:
                p_qk(0, r)
                p_qk(1, r)
                for u in range(16):
                    p_turn(u, r)
                    if u + 2 < 16:
                        p_qk(u + 2, r)
                    if u:
                        p_pv(u - 1, r)
                p_pv(15, r)

            def k_turn(h, i, c):
                pe.wait_ge(t_ke, 5 * h + c + 1 + 10 * i)
                if c in (0, 2):
                    pe.wait_ge(s_sg[2 * h + c // 2], 16 + 16 * i)
                if c == 4:
                    pe.wait_ge(s_wb[h], 16 + 16 * i)
                kp = (h + c) % 2
                for a in range(2):
                    for j in range(4):
                        src = sg[2 * h + c // 2][:, 4 * (c % 2) + j, a * P:(a + 1) * P] if c < 4 else wb[h][:, j, a * P:(a + 1) * P]
                        last = nc.tensor.transpose(ps[:, 2 * kp + a, j * P:(j + 1) * P], src, ident[:, :])
                last.then_inc(t_kt, 1)

            def k_qk(h, i, c):
                if c == 0:
                    pe.wait_ge(t_qb, h + 1 + 2 * i)
                if c < 5:
                    pe.wait_ge(t_ke, 5 * h + c + 3 + 10 * i)
                pe.wait_ge(t_se, 6 * h + c + 1 + 12 * i)
                for m in range(1 if c < 5 else 2):
                    for a in range(2):
                        if c < 5:
                            out, keys = ps[:, 4, :], kT[(h + c) % 2][:, a, :]
                        else:
                            out, keys = ps[:, 4, m * TS:(m + 1) * TS], kn[:, m, a, bass.ds(16 * i + TS * h, TS)]
                        last = nc.tensor.matmul(out, sq_[h][:, a, :], keys, start=(a == 0), stop=(a == 1))
                last.then_inc(t_qk, 1)

            def s_turn(h, i, g):
                if g == 0:
                    pe.wait_ge(t_sc, h + 1 + 2 * i)
                pe.wait_ge(t_pe, 6 * h + g + 1 + 12 * i)
                bank = 5 + 2 * (g % 2)
                if g < 5:
                    for x in range(4):
                        c0 = (4 * g + x) * P + (TS if g == 4 else 0)
                        last = nc.tensor.transpose(ps[:, bank, x * P:(x + 1) * P], sS[h][:, c0:c0 + P], ident[:, :])
                else:
                    for m, c0 in enumerate((PAST, PAST + TS + WIN)):
                        last = nc.tensor.transpose(ps[0:TS, bank, m * P:(m + 1) * P], sS[h][:, c0:c0 + TS], ident[:, :])
                last.then_inc(t_pt, 1)

            def s_pvs(h, i, g):
                if g == 0:
                    pe.wait_ge(t_of, h + 1 + 2 * i)
                if g == 5:
                    pe.wait_ge(s_vn[h], 32 + 32 * i)
                pe.wait_ge(t_pe, 6 * h + g + 3 + 12 * i)
                for x in range(4 if g < 5 else 2):
                    for a in range(2):
                        cols = slice(G * HD + a * P, G * HD + (a + 1) * P)
                        if g < 4:
                            v, p = sg[2 * h + g // 2][:, 4 * (g % 2) + x, cols], sT[:, 4 * g + x, a * HD:(a + 1) * HD]
                        elif g == 4:
                            v, p = wb[h][:, x, cols], sT[:, 16 + x, a * HD:(a + 1) * HD]
                        else:
                            v, p = vn[h][:, x, a * P:(a + 1) * P], sT[0:TS, 20 + x, a * HD:(a + 1) * HD]
                        last = nc.tensor.matmul(ps[:, 6, a * HD:(a + 1) * HD], v, p, start=(g == 0 and x == 0 and a == 0),
                                                stop=(g == 5 and x == 1), skip_group_check=True)
                last.then_inc(t_pv, 1)

            def pe_phase(k, p):
                for c in range(5):
                    if k:
                        k_turn(*k, c)
                        if c:
                            k_qk(*k, c - 1)
                    if p and c == 3:
                        s_turn(*p, 0)
                    if p and c == 4:
                        s_turn(*p, 1)
                        s_pvs(*p, 0)
                if k:
                    k_qk(*k, 4)
                    k_qk(*k, 5)
                for g in range(2, 6):
                    if p:
                        s_turn(*p, g)
                        s_pvs(*p, g - 1)
                if p:
                    s_pvs(*p, 5)

            pe.sem_inc(t_qk, 12)
            pe.sem_inc(t_pv, 12)
            pe.sem_inc(t_pt, 12)
            pe_phase((0, 0), None)
            with pe.Fori(0, NB // 2 - 1) as i:
                pe_phase((1, i), (0, i))
                pe_phase((0, i + 1), (1, i))
            pe_phase((1, NB // 2 - 1), (0, NB // 2 - 1))
            pe_phase(None, (1, NB // 2 - 1))

            pe.wait_ge(s_mlo, KT)
            with pe.Fori(0, KT // 2) as i:
                for u in range(2):
                    gemm(S_OUT + u, 2 * i, (mix_hi, mix_lo))

            def norm_pe(turn, steps):
                pe.wait_ge(s_acc, 2 + steps)
                for k in range(KT):
                    for h in range(2):
                        last = nc.tensor.matmul(ps[:, 4 + h, 0:TH], means[:, :], h_t[:, k, h * TH:(h + 1) * TH], start=(k == 0), stop=(k == KT - 1))
                last.then_inc(l_mean, 1)
                for k in range(KT):
                    pe.wait_ge(l_sq, KT * turn + k + 1)
                    for h in range(2):
                        last = nc.tensor.matmul(ps[:, 6 + h, 0:TH], means[:, :], sqr[k % 2][:, h * TH:(h + 1) * TH], start=(k == 0), stop=(k == KT - 1))
                    last.then_inc(l_acc, 1)

            pe.sem_inc(l_acc, 2)
            norm_pe(0, S_MLP)

            pe.wait_ge(l_al, KT)

            def chunk_pe(c):
                with pe.Fori(0, CT // 2) as i:
                    for u in range(2):
                        gemm(S_MLP + u, 16 * c + 2 * i, (h_hi, h_lo))
                with pe.Fori(0, CT // 2) as i:
                    for u in range(2):
                        pe.wait_ge(f_l, 2 + CT + 8 * c)
                        gemm(S_MLP + CT + u, 16 * c + 2 * i, (f_hi, f_lo), kts=CT, tiles=2)

            with pe.Fori(0, NCHUNK) as c:
                chunk_pe(c)
            norm_pe(1, END)
            pe.wait_ge(l_aff, 2 * KT)
            for t in range(PT_TOK + 1):
                n = P if t < PT_TOK else TN
                if t >= 2:
                    pe.wait_ge(o_cp, t - 1)
                for k in range(KT):
                    last = nc.tensor.transpose(ps[0:n, 4 * (t % 2) + k // 4, (k % 4) * P:(k % 4 + 1) * P], h_t[:, k, t * P:t * P + n], ident[:, :])
                last.then_inc(o_tr, 1)


_INS = ["x_prompt", "x_sample", "cache_cmp", "cache_slc", "cache_win", "state_conv", "page_table", "w_in",
        "w_cmp_k", "w_cmp_v", "conv_w", "w_out", "ln1_g", "ln1_b", "w_mlp1", "w_mlp2", "ln2_g", "ln2_b"]
_OUTS = [(1, TP, D), (NB, TS, D), (1, 1, TP, 2, G, HD), (1, 1, TP, 2, G, HD), (1, 1, TP, 2, G, HD), (1, 1, 2, CONV),
         (1, NB, TS, 2, G, HD), (1, NB, TS, 2, G, HD), (1, NB, WIN, 2, G, HD), (1, NB, 2, CONV)]


def kernel(**inputs):
    import concourse.bacc as bacc
    from concourse.bass_utils import run_bass_kernel_spmd

    nc = bacc.Bacc("TRN2", target_bir_lowering=False, num_devices=1)
    arrays, args = {}, []
    for name in _INS:
        a = np.ascontiguousarray(inputs[name])
        arrays[f"in_{name}"] = a
        args.append(nc.dram_tensor(f"in_{name}", a.shape, mybir.dt.from_np(a.dtype), kind="ExternalInput").ap())
    for i, shape in enumerate(_OUTS):
        args.append(nc.dram_tensor(f"out_{i}", shape, F32, kind="ExternalOutput").ap())
    build(nc, *args)
    r = run_bass_kernel_spmd(nc, [arrays], core_ids=[0])
    return tuple(r.results[0][f"out_{i}"] for i in range(len(_OUTS)))
```

```python
from contextlib import ExitStack

import numpy as np

import concourse.bass as bass
from concourse import mybir

ALU = mybir.AluOpType
ACT = mybir.ActivationFunctionType
AX = mybir.AxisListType
F32 = mybir.dt.float32
F32R = mybir.dt.float32r
I32 = mybir.dt.int32
U32 = mybir.dt.uint32

P = 128
D = 2048
TP = 512
NB, TS = 8, 8
TN = NB * TS
T = TP + TN
TH = T // 2
PAGE, NPAGE = 128, 16
PAST = PAGE * NPAGE
WIN = 512
HD = 64
G, R = 4, 4
BLK = 64
NBLK = PAST // BLK
PBLK = TP // BLK
NSEL = 16
FORCED = 3
CONV = 1024
FF = 8192
EPS = 1e-5
NEG = -1e30
SCALE = HD ** -0.5
ALPHA = 2.0 ** 0.25

KT = D // P
PT_TOK = TP // P
C_Q, C_KV, C_G, C_XIN = 0, 1024, 2560, 2608
C_BG, C_CG = C_XIN + CONV, C_XIN + 2 * CONV
NG = 3 * G * R
NKV = 12
KV_CMP, KV_SLC, KV_WIN = 0, 4, 8
NCONV = CONV // P

S_GATE = 0
S_CONV = 1
S_Q = S_CONV + 3 * NCONV
S_KV = S_Q + 8
S_OUT = S_KV + NKV
S_MLP = S_OUT + KT
CHUNK = 1024
NCHUNK = FF // CHUNK
CT = CHUNK // P
END = S_MLP + NCHUNK * 2 * CT
P_GROUPS = ((), (), (0,), (1, 2), (3, 4), (5,))
P_GROUPS_LAST = ((), (), (0,), (1,), (), (2, 3, 4, 5))
RAW_OUT_DMAS = 5

UNIT_TILE = (0, 3, 0, 3, 1, 2, 1, 2)
UNIT_HEAD = (0, 0, 1, 1, 0, 0, 1, 1)

GROW = 8
GSEQ = P * GROW
NGATH = NB * PAST // GSEQ
XU = 4 * (PT_TOK + 1)
UNITS = PT_TOK * G * R
ROWW = 2 * G * HD


class Chain:

    def __init__(self, eng, sem):
        self.eng, self.sem, self.n, self.loop = eng, sem, 0, 0

    def __call__(self, ins):
        ins.then_inc(self.sem, 1)
        self.n += 1
        return self

    def wait(self):
        self.eng.wait_ge(self.sem, self.loop + self.n)

    def turns(self, count, per_turn):
        start, outer = self.n, self.loop
        with self.eng.Fori(0, count) as i:
            self.loop = outer + i * per_turn
            yield i
            assert self.n == start + per_turn, (self.n - start, per_turn)
        self.n, self.loop = start + per_turn * count, outer


DMAS = [2] * S_OUT + [RAW_OUT_DMAS] * KT + [2] * (END - S_MLP)


def raw_in(s, pairs=0):
    fixed = 16 * sum(DMAS[x] for x in range(s + 1) if x % 2 == s % 2)
    return fixed + pairs * (16 * DMAS[s])


def build(nc, x_prompt, x_sample, cache_cmp, cache_slc, cache_win, state_conv, page_table, w_in, w_cmp_k,
          w_cmp_v, conv_w, w_out, ln1_g, ln1_b, w_mlp1, w_mlp2, ln2_g, ln2_b,
          y_prompt, y_sample, new_cmp_prompt, new_slc_prompt, new_win_prompt, new_conv_prompt,
          new_cmp_sample, new_slc_sample, new_win_sample, new_conv_sample):
    ctx = ExitStack()
    with ctx:
        def sem(name):
            return ctx.enter_context(nc.semaphore(name))

        base = -(-nc.sbuf_base // 64) * 64
        W0 = base
        A0 = W0 + 6 * 8192
        B0 = A0 + 2 * KT * T * 4
        C0 = B0 + (8 + NKV) * T * 4
        K0 = C0 + KT * T * 4
        fixed = [K0]

        def at(name, offset, shape, dt=F32):
            return nc.alloc_sbuf_tensor_at(name, shape, dt, offset=offset)

        def const(name, shape, dt=F32):
            t = at(name, fixed[0], shape, dt)
            fixed[0] += -(-int(np.prod(shape[1:])) * 4 // 32) * 32
            assert fixed[0] <= nc.sbuf_usable_end, (name, fixed[0], nc.sbuf_usable_end)
            return t

        w_raw = [at(f"w_raw{i}", W0 + 8192 * i, [P, 2048]) for i in range(2)]
        w_hi = [at(f"w_hi{i}", W0 + 8192 * (2 + i), [P, 2048], F32R) for i in range(2)]
        w_lo = [at(f"w_lo{i}", W0 + 8192 * (4 + i), [P, 2048], F32R) for i in range(2)]
        x_hi = at("x_hi", A0, [P, KT, T], F32R)
        x_lo = at("x_lo", A0 + KT * T * 4, [P, KT, T], F32R)
        x_rows = at("x_rows", B0, [P, PT_TOK + 1, D])
        gath = [at(f"gath{i}", B0 + 16384 * i, [P, GROW, ROWW]) for i in range(2)]
        wcmp = at("wcmp", B0 + 32768, [P, 2, GROW, HD])
        part = [at(f"part{i}", B0 + 36864 + 2048 * i, [P, ROWW]) for i in range(2)]
        q_t = at("q_t", B0, [P, R, 2, T])
        kv_t = at("kv_t", B0 + 8 * T * 4, [P, NKV, T])
        x_t = at("x_t", C0, [P, KT, T])
        mix = at("mix", C0, [P, KT, T])
        xin = at("xin", C0, [P, T])
        ZW = 2 + TP + NB * (2 + TS)
        zpad = at("zpad", C0 + 2304, [P, ZW])
        fir = at("fir", C0 + 4736, [P, ZW])
        cmp_t0 = at("cmp_t0", C0 + 7168, [P, NB, 4, NBLK])
        gates0 = at("gates0", C0 + 11264, [P, T])
        st_in = at("st_in", A0, [2 * NB, CONV])
        zl_rows = at("zl_rows", C0, [2 + 2 * NB, CONV])

        kvn = at("kvn", W0, [P, PT_TOK + 1, NKV * P])
        qbd = at("qbd", W0 + 30720, [P, NB, 2, P])
        cmp_t = at("cmp_t", W0 + 38912, [P, NB, 4, NBLK])
        causal = at("causal", W0 + 43008, [P, 2 * TP - P])
        same = at("same", W0 + 46592, [P, P])
        tok_of = at("tok_of", W0 + 47104, [P, TS])
        grp_of = at("grp_of", W0 + 47136, [P, G])
        pair_of = at("pair_of", W0 + 47168, [P, 2 * R * 2])
        before = at("before", W0 + 47232, [P, TS])
        gn = at("gn", W0 + 47264, [P, PT_TOK, NG])
        gs = at("gs", W0 + 48032, [P, 3, NB])
        mb = at("mb", W0 + 48128, [P, NB, NBLK])
        nmask = at("nmask", W0 + 49152, [P, 2, TS])
        wmask = at("wmask", W0 + 49216, [P, TP])
        kn = at("kn", W0 + 51264, [P, 2, 2, TN])
        X0 = W0 + 53312
        tri = at("tri", C0 + 4736, [P, P // TS, TS])
        gexp = at("gexp", C0 + 5248, [NG, 3, P])
        gtmp = at("gtmp", X0 + 2048, [P, 3, TN])
        tmp = at("tmp", C0 + 13568, [P, 2, PBLK, BLK])
        kc = at("kc", C0 + 7040, [P, 4, PBLK])
        kbd = at("kbd", C0 + 6784, [P, 2, 2 * PBLK])
        e8 = at("e8", X0 + 11520, [PBLK, P])
        vcn = at("vcn", X0 + 12032, [PBLK, G * HD])
        vbd = at("vbd", X0 + 14080, [P, 2 * R, P])
        sc = at("sc", X0 + 18176, [P, PT_TOK, P])
        cbias = at("cbias", C0 + 6912, [P, PT_TOK, PBLK])
        st1 = at("st1", X0 + 20352, [P, PT_TOK * 16])
        st2 = at("st2", X0 + 20608, [P, PT_TOK * 16])
        pct = at("pct", X0 + 20864, [P, TP])
        ss = at("ss", X0 + 22912, [P, NB, NBLK])
        pg = at("pg", X0 + 23936, [P, NB, NBLK])
        vals = at("vals", X0 + 24960, [P, NB, 40])
        st3 = at("st3", X0 + 26304, [P, NB])
        st4 = at("st4", X0 + 26336, [P, NB])
        m8 = at("m8", X0 + 38656, [P, NB, 8])
        m5 = at("m5", X0 + 38912, [P, NB, 8])
        pcts = at("pcts", X0 + 26368, [NBLK, NB, P])
        vcs = at("vcs", X0 + 30464, [NBLK, NB, 2, P])
        pS = [at(f"pS{i}", X0 + 4096 * i, [P, 2, TP]) for i in range(4)]
        pT = [at(f"pT{i}", X0 + 16384 + 4096 * i, [P, 8, P]) for i in range(2)]
        pq = [at(f"pq{i}", X0 + 24576 + 2048 * i, [P, TP]) for i in range(2)]
        pst = [at(f"pst{i}", X0 + 28672 + 64 * i, [P, 3, 2]) for i in range(4)]
        NS_COLS = PAST + TS + WIN + TS
        sg = [at(f"sg{i}", X0 + 16384 * ((i + 2) % 4), [P, GROW, ROWW]) for i in range(4)]
        assert X0 + 65536 <= B0
        wb = [at(f"wb{i}", W0 + 8192 * (1 - i), [P, WIN // P, ROWW]) for i in range(2)]
        sS = [at("sS0", W0 + 16384, [P, NS_COLS]), at("sS1", B0, [P, NS_COLS])]
        vn = [at(f"vn{i}", B0 + 10304 + 2048 * i, [TS, 2, G * HD]) for i in range(2)]
        kT = [at(f"kT{i}", B0 + 14400 + 4096 * i, [P, 2, 512]) for i in range(2)]
        NPB = 22
        sT = at("sT", B0 + 22592, [P, NPB, P])
        sq_ = [at(f"qb{i}", B0 + 33856 + 1024 * i, [P, 2, P]) for i in range(2)]
        sst = [at(f"sst{i}", B0 + 35904 + 64 * i, [P, 3, 2]) for i in range(2)]
        smx = [at(f"smx{i}", B0 + 36032 + 64 * i, [P, 8]) for i in range(2)]
        mix_hi = at("mix_hi", A0, [P, KT, T], F32R)
        mix_lo = at("mix_lo", A0 + KT * T * 4, [P, KT, T], F32R)
        h_hi = at("h_hi", A0, [P, KT, T], F32R)
        h_lo = at("h_lo", A0 + KT * T * 4, [P, KT, T], F32R)
        x_r = at("x_r", B0, [P, KT, T])
        h_t = at("h_t", C0, [P, KT, T])
        f_hi = at("f_hi", B0, [P, CT, T], F32R)
        f_lo = at("f_lo", B0 + CT * T * 4, [P, CT, T], F32R)
        Y0 = B0 + KT * T * 4
        sqr = [at(f"sqr{i}", Y0 + 2304 * i, [P, T]) for i in range(2)]
        rstd = at("rstd", Y0 + 4608, [P, T])
        rl = [at(f"rl{i}", Y0 + 2304 * i, [P, T]) for i in range(2)]
        fs = [at(f"fs{i}", Y0 + 4608 + 2304 * i, [P, T]) for i in range(2)]
        o_rows = [at(f"o_rows{i}", A0 + 8192 * i, [P, D]) for i in range(PT_TOK + 1)]

        ident = const("ident", [P, P])
        means = const("means", [P, P])
        sel8 = const("sel8", [P, P // GROW])
        pars = const("pars", [88, P])
        pars_t = const("pars_t", [P, 88])
        st_t = const("st_t", [P, NCONV, NB, 2])
        zlast = const("zlast", [P, NCONV, 2 + 2 * NB])
        pt_i = const("pt_i", [NPAGE // 2, 2 * NB], I32)
        pt_f = const("pt_f", [NPAGE // 2, 2 * NB])
        w_of = const("w_of", [NPAGE // 2, 1])
        spread = const("spread", [NPAGE // 2, P])
        p_of = const("p_of", [P, 1])
        idx = const("idx", [P, NGATH], U32)
        idx1 = [const(f"idx1{i}", [P, 1], U32) for i in range(4)]
        h_sum = const("h_sum", [P, T])
        w_rows = at("w_rows", A0 + 4096, [BLK, 4 * HD])
        wt = const("wt", [P, 2, BLK])
        LN1G, LN1B, LN2G, LN2B, CW = 0, KT, 2 * KT, 3 * KT, 4 * KT

        ps = ctx.enter_context(nc.psum_tensor("ps", [P, 8, 512], F32))

        def banks(a, n, cols):
            return ps[:, a:a + n, 0:cols]

        def flat(a, cols, rows=P):
            return ps[0:rows, a:a + 2, :].rearrange("p b c -> p (b c)")[:, 0:cols]

        x_dram = nc.dram_tensor("x_scratch", [P, KT * T], F32).ap()
        cmp_rows = cache_cmp.rearrange("o n (s j) c g d -> (o n s) (j c g d)", j=GROW)
        slc_rows = cache_slc.rearrange("o n (s j) c g d -> (o n s) (j c g d)", j=GROW)
        w_in_v = w_in[0].rearrange("(kt p) n -> p kt n", p=P)
        w_q_v = w_in[0][:, C_Q:C_Q + 1024].rearrange("(kt p) (a gl r d) -> p kt a gl r d", p=P, a=2, gl=2, r=R)

        s_par = sem("s_par")
        s_x = [sem(f"s_x{t}") for t in range(PT_TOK + 1)]
        s_asked, s_wcmp, s_pt, s_idx = sem("s_asked"), sem("s_wcmp"), sem("s_pt"), sem("s_idx")
        s_const = sem("s_const")
        s_w = [sem(f"s_w{i}") for i in range(2)]
        s_hi, s_lo, s_gemm, s_acc = sem("s_hi"), sem("s_lo"), sem("s_gemm"), sem("s_acc")
        s_tr = sem("s_tr")
        s_pre = sem("s_pre")
        s_xt, s_xhi, s_xlo, s_xsave = sem("s_xt"), sem("s_xhi"), sem("s_xlo"), sem("s_xsave")
        s_gath = [sem(f"s_gath{i}") for i in range(2)]
        s_idx1, s_gfree, s_part, s_sel, s_cmpv = sem("s_idx1"), sem("s_gfree"), sem("s_part"), sem("s_sel"), sem("s_cmpv")
        s_gate, s_vmul, s_xtd = sem("s_gate"), sem("s_vmul"), sem("s_xtd")
        s_wr = sem("s_wr")
        s_kvT, s_kvn, s_kvout = sem("s_kvT"), sem("s_kvn"), sem("s_kvout")
        s_one, s_b, s_a = sem("s_one"), sem("s_b"), sem("s_a")
        s_mask = sem("s_mask")
        s_q, s_qk, s_mx, s_ex, s_sc, s_pt_, s_pe, s_pv, s_of = (sem(n) for n in
            ("s_q", "s_qk", "s_mx", "s_ex", "s_sc", "s_ptr", "s_pe", "s_pv", "s_of"))
        s_sg = [sem(f"s_sg{i}") for i in range(4)]
        s_wb, s_vn = [sem(f"s_wb{i}") for i in range(2)], [sem(f"s_vn{i}") for i in range(2)]
        t_i, t_qb, t_kt, t_ke, t_qk, t_se, t_mx, t_ex, t_sc, t_pt, t_pe, t_pv, t_of = (sem(n) for n in
            ("t_i", "t_qb", "t_kt", "t_ke", "t_qk", "t_se", "t_mx", "t_ex", "t_sc", "t_pt", "t_pe", "t_pv", "t_of"))
        s_mhi, s_mlo, s_xr = sem("s_mhi"), sem("s_mlo"), sem("s_xr")
        l_mean, l_sub, l_sq, l_acc, l_eps, l_sd, l_mul, l_aff, l_lo = (sem(n) for n in
            ("l_mean", "l_sub", "l_sq", "l_acc", "l_eps", "l_sd", "l_mul", "l_aff", "l_lo"))
        l_sum = sem("l_sum")
        f_rl, f_f, f_h, f_l = sem("f_rl"), sem("f_f"), sem("f_h"), sem("f_l")
        o_tr, o_cp = sem("o_tr"), [sem(f"o_cp{i}") for i in range(2)]
        s_dve, s_pool = sem("s_dve"), sem("s_pool")
        s_zlT, s_zlv, s_zout, s_out = sem("s_zlT"), sem("s_zlv"), sem("s_zout"), sem("s_out")

        block = ctx.enter_context(nc.Block())

        def times_cmp(eng, v, m):
            rows = gath[v][:, :, m * G * HD:(m + 1) * G * HD].rearrange("p j (g d) -> p j g d", g=G)
            return eng.tensor_tensor(rows, rows, wcmp[:, m, :, :].unsqueeze(2).broadcast_to([P, GROW, G, HD]), ALU.mult)

        @block.sync
        def _(sp):
            for row, ap in ((LN1G, ln1_g), (LN1B, ln1_b), (LN2G, ln2_g), (LN2B, ln2_b)):
                sp.dma_start(pars[row:row + KT, :], ap.rearrange("o (k p) -> (o k) p", p=P)).then_inc(s_par, 16)
            sp.dma_start(pars[CW:CW + 3 * NCONV, :], conv_w.rearrange("o j (c p) -> (o j c) p", p=P)).then_inc(s_par, 16)
            sp.dma_start(st_in[:, :], state_conv.rearrange("o b j n -> (o b j) n")).then_inc(s_par, 16)
            sp.dma_start(pt_i[:, :], page_table.rearrange("b (h w) -> w (b h)", w=NPAGE // 2),
                         allow_slow_non_contiguous=True).then_inc(s_par, 16)
            for m in range(4):
                sp.dma_start(w_rows[:, m * HD:(m + 1) * HD], (w_cmp_k, w_cmp_v)[m // 2][0]).then_inc(s_wr, 16)
            def load(s, halves, it=0):
                if s >= 2 or not isinstance(it, int):
                    sp.wait_ge(s_lo, s - 1 + it)
                for dst, src in halves:
                    sp.dma_start(dst, src).then_inc(s_w[s % 2], 16)

            def by_k(s, src):
                _, kt, n = src.shape
                dst = w_raw[s % 2][:, :].rearrange("p (k n) -> p k n", n=n)
                return [(dst[:, h:h + kt // 2, :], src[:, h:h + kt // 2, :]) for h in (0, kt // 2)]

            def q_halves(s, a, r):
                dst = w_raw[s % 2][:, :].rearrange("p (k gl n) -> p k gl n", gl=2, n=HD)
                return [(dst[:, :, gl, :], w_q_v[:, :, a, gl, r, :]) for gl in range(2)]

            def conv_cols(u, c):
                return w_in_v[:, :, bass.ds((C_XIN, C_CG, C_BG)[u] + c * P, P)]

            load(S_GATE, by_k(0, w_in_v[:, :, C_G:C_G + P]))
            for t in range(PT_TOK):
                sp.dma_start(x_rows[:, t, :], x_prompt[0, t * P:(t + 1) * P, :]).then_inc(s_x[t], 16)
            sp.dma_start(x_rows[0:TN, PT_TOK, :], x_sample.rearrange("b t d -> (b t) d")).then_inc(s_x[PT_TOK], 16)
            load(S_CONV, by_k(1, conv_cols(0, 0)))
            sp.wait_ge(s_tr, XU)
            for m, wc in enumerate((w_cmp_k, w_cmp_v)):
                sp.dma_start(wcmp[:, m, :, :].rearrange("p j d -> p (j d)"),
                             wc[0].rearrange("(s j) d -> s (j d)", s=GROW).unsqueeze(0).broadcast_to([P // GROW, GROW, GROW * HD])
                             ).then_inc(s_wcmp, 16)
            load(S_CONV + 1, by_k(S_CONV + 1, conv_cols(1, 0)))
            sp.wait_ge(s_xt, 3 * (PT_TOK + 1))
            sp.wait_ge(s_xtd, PT_TOK + 1)
            sp.dma_start(x_dram, x_t[:, :, :].rearrange("p k t -> p (k t)")).then_inc(s_xsave, 16)
            for u in range(2, 6):
                load(S_CONV + u, by_k(S_CONV + u, conv_cols(u % 3, u // 3)))
            with sp.Fori(1, NCONV // 2) as i:
                for u in range(6):
                    load(S_CONV + u, by_k(S_CONV + u, conv_cols(u % 3, 2 * i + u // 3)), it=6 * i)
            with sp.Fori(0, R) as r:
                for a in range(2):
                    load(S_Q + a, q_halves(S_Q + a, a, r), it=2 * r)
            with sp.Fori(0, NKV // 2) as i:
                for u in range(2):
                    load(S_KV + u, by_k(S_KV + u, w_in_v[:, :, bass.ds(C_KV + u * P + i * (2 * P), P)]), it=2 * i)

            sp.wait_ge(s_zlv, 1)
            sp.dma_start(new_conv_prompt.rearrange("o b j n -> (o b j) n"), zl_rows[0:2, :]).then_inc(s_zout, 16)
            sp.dma_start(new_conv_sample.rearrange("o b j n -> (o b j) n"), zl_rows[2:2 + 2 * NB, :]).then_inc(s_zout, 16)
            for t in range(PT_TOK):
                sp.wait_ge(s_kvn, t + 1)
                for m, out in ((KV_CMP, new_cmp_prompt), (KV_SLC, new_slc_prompt), (KV_WIN, new_win_prompt)):
                    sp.dma_start(out[0, 0].rearrange("t c g d -> t (c g d)")[t * P:(t + 1) * P, :],
                                 kvn[:, t, m * P:m * P + ROWW]).then_inc(s_kvout, 16)
            sp.wait_ge(s_kvn, PT_TOK + 1)
            for m, out in ((KV_CMP, new_cmp_sample), (KV_SLC, new_slc_sample)):
                sp.dma_start(out[0].rearrange("b t c g d -> (b t) (c g d)"), kvn[0:TN, PT_TOK, m * P:m * P + ROWW]).then_inc(s_kvout, 16)
            sp.dma_start(new_win_sample[0].rearrange("b t c g d -> b t (c g d)")[:, WIN - TS:WIN, :],
                         kvn[0:TN, PT_TOK, KV_WIN * P:KV_WIN * P + ROWW]).then_inc(s_kvout, 16)

            keep_rows = WIN - TS
            sp.dma_start(new_win_sample[0].rearrange("b (x y) c g d -> x b (y c g d)", y=4)[0:keep_rows // 4],
                         cache_win[0].rearrange("b (x y) c g d -> x b (y c g d)", y=4)[TS // 4:WIN // 4]).then_inc(s_out, 16)
            win_rows = cache_win[0].rearrange("b (p j) c g d -> p b (j c g d)", p=P)
            new_slc = new_slc_sample[0].rearrange("b t c g d -> t b c (g d)")
            new_win = new_win_sample[0].rearrange("b t c g d -> t b c (g d)")
            sp.wait_ge(s_kvout, 16 * (3 * PT_TOK + 3))
            sp.wait_ge(s_pv, 2 + UNITS)
            sp.wait_ge(s_of, 2 * R + 2)

            def load_window(h, i):
                sp.wait_ge(t_pv, 6 * h + 6 + 12 * i)
                sp.dma_start(wb[h][:, :, :].rearrange("p j c -> p (j c)"),
                             win_rows[:, bass.ds(2 * i + h, 1), :].rearrange("p b x -> p (b x)")).then_inc(s_wb[h], 16)
                for m, rows in ((0, new_slc[:, :, 1, :]), (1, new_win[WIN - TS:WIN, :, 1, :])):
                    sp.dma_start(vn[h][:, m, :], rows[:, bass.ds(2 * i + h, 1), :].rearrange("t b x -> t (b x)")).then_inc(s_vn[h], 16)

            with sp.Fori(0, NB // 2) as i:
                for h in range(2):
                    load_window(h, i)

            w_att_v = w_out[0][0:CONV, :].rearrange("(a gl r d) n -> a gl d r n", a=2, gl=2, r=R)
            w_cnv_v = w_out[0][CONV:2 * CONV, :].rearrange("(k p) n -> p k n", p=P)

            def out_loads(s, i, u):
                n = bass.ds(i * (2 * P) + u * P, P)
                dst = w_raw[s % 2]
                loads = [(dst[gl * HD:(gl + 1) * HD, 0:CONV].rearrange("p (r a n) -> p r a n", r=R, a=2)[:, :, a, :],
                          w_att_v[a, gl][:, :, n]) for a in range(2) for gl in range(2)]
                return loads + [(dst[:, CONV:2 * CONV].rearrange("p (k n) -> p k n", n=P), w_cnv_v[:, :, n])]

            sp.wait_ge(t_pv, 12 + 6 * (NB - 1))
            load(S_OUT, out_loads(S_OUT, 0, 0))
            sp.wait_ge(t_of, 1 + NB)
            load(S_OUT + 1, out_loads(S_OUT + 1, 0, 1))
            sp.dma_start(x_r[:, :, :].rearrange("p k t -> p (k t)"), x_dram).then_inc(s_xr, 16)
            with sp.Fori(1, KT // 2) as i:
                for u in range(2):
                    load(S_OUT + u, out_loads(S_OUT + u, i, u), it=2 * i)
            w1_v = w_mlp1[0].rearrange("(k p) n -> p k n", p=P)
            w2_v = w_mlp2[0].rearrange("(c k p) n -> p c k n", p=P, k=CT)
            with sp.Fori(0, NCHUNK) as c:
                with sp.Fori(0, CT // 2) as i:
                    for u in range(2):
                        load(S_MLP + u, by_k(S_MLP + u, w1_v[:, :, bass.ds(c * CHUNK + i * (2 * P) + u * P, P)]), it=16 * c + 2 * i)
                with sp.Fori(0, CT // 2) as i:
                    for u in range(2):
                        load(S_MLP + CT + u, by_k(S_MLP + CT + u,
                             w2_v[:, bass.ds(c, 1), :, bass.ds(i * (4 * P) + u * 2 * P, 2 * P)].rearrange("p c k n -> p (c k) n")),
                             it=16 * c + 2 * i)

            for n in range(XU):
                q, t = n // (PT_TOK + 1), n % (PT_TOK + 1)
                cols = slice(q * 512, (q + 1) * 512)
                sp.wait_ge(o_cp[n % 2], n // 2 + 1)
                if t < PT_TOK:
                    sp.dma_start(y_prompt[0, t * P:(t + 1) * P, cols], o_rows[t][:, cols]).then_inc(s_out, 16)
                else:
                    sp.dma_start(y_sample.rearrange("b t d -> (b t) d")[:, cols], o_rows[t][0:TN, cols]).then_inc(s_out, 16)
            sp.wait_ge(s_out, 16 * (1 + XU))
            sp.wait_ge(s_zout, 32)

        @block.gpsimd
        def _(pool):
            pc = Chain(pool, s_pool)
            pc(nc.gpsimd.memset(ident[:, :], 0.0))
            pc(nc.gpsimd.memset(means[:, :], 1.0 / D))
            pc(nc.gpsimd.memset(sel8[:, :], 1.0))
            pc(nc.gpsimd.memset(spread[:, :], 1.0))
            pc.wait()
            pc(nc.gpsimd.affine_select(out=ident[:, :], in_=ident[:, :], compare_op=ALU.not_equal, fill=1.0,
                                       base=0, pattern=[[-1, P]], channel_multiplier=1))
            pc(nc.gpsimd.affine_select(out=sel8[:, :], in_=sel8[:, :], compare_op=ALU.is_ge, fill=0.0,
                                       base=0, pattern=[[-GROW, P // GROW]], channel_multiplier=1))
            pc(nc.gpsimd.affine_select(out=spread[:, :], in_=spread[:, :], compare_op=ALU.is_ge, fill=0.0,
                                       base=0, pattern=[[1, P]], channel_multiplier=-16))
            pc.wait()
            pc(nc.gpsimd.affine_select(out=sel8[:, :], in_=sel8[:, :], compare_op=ALU.is_ge, fill=0.0,
                                       base=GROW - 1, pattern=[[GROW, P // GROW]], channel_multiplier=-1))
            pc(nc.gpsimd.affine_select(out=spread[:, :], in_=spread[:, :], compare_op=ALU.is_ge, fill=0.0,
                                       base=15, pattern=[[-1, P]], channel_multiplier=16))
            pc(nc.gpsimd.iota(p_of[:, :], pattern=[[0, 1]], base=0, channel_multiplier=1,
                              allow_small_or_imprecise_dtypes=True))
            pc(nc.gpsimd.iota(w_of[:, :], pattern=[[0, 1]], base=0, channel_multiplier=1,
                              allow_small_or_imprecise_dtypes=True))
            pc.wait()
            pool.sem_inc(s_const, 1)

            pool.wait_ge(s_tr, XU)
            pool.wait_ge(s_idx, 1)
            pool.wait_ge(s_wcmp, 32)
            def cmp_gather(i, v):
                slot = v % 2
                pool.wait_ge(s_gfree, 1 + v + 2 * i)
                nc.gpsimd.tensor_copy(idx1[slot][:, :], idx[:, bass.ds(2 * i + v, 1)]).then_inc(s_idx1, 1)
                pool.wait_ge(s_idx1, 1 + v + 2 * i)
                pool.sem_inc(s_asked, 1)
                nc.gpsimd.indirect_dma_start(
                    gath[slot][:, :, :].rearrange("p j c -> p (j c)"), None, cmp_rows,
                    bass.IndirectOffsetOnAxis(ap=idx1[slot][:, 0:1], axis=0)).then_inc(s_gath[slot], 16)

            def cmp_v(i, v):
                pool.wait_ge(s_gath[v], 16 + 16 * i)
                times_cmp(nc.gpsimd, v, 1).then_inc(s_vmul, 1)

            cmp_gather(0, 0)
            with pool.Fori(0, NGATH // 2 - 1) as i:
                for v in range(2):
                    cmp_gather(i, v + 1)
                    cmp_v(i, v)
            cmp_gather(NGATH // 2 - 1, 1)
            cmp_v(NGATH // 2 - 1, 0)
            cmp_v(NGATH // 2 - 1, 1)

            pool.wait_ge(s_acc, 2 + S_Q)
            pc(nc.gpsimd.memset(tri[:, :, :], 1.0))
            pc(nc.gpsimd.memset(gexp[:, :, :], 0.0))
            pc(nc.gpsimd.memset(kbd[:, :, :], 0.0))
            pc(nc.gpsimd.memset(cbias[:, :, :], 0.0))
            pc.wait()
            pc(nc.gpsimd.affine_select(out=tri[:, :, :], in_=tri[:, :, :], compare_op=ALU.is_ge, fill=0.0,
                                       base=0, pattern=[[-TS, P // TS], [0, TS]], channel_multiplier=1))
            for br in range(3):
                pc(nc.gpsimd.affine_select(out=gexp[:, br, :].rearrange("c (h t) -> c h t", t=TS),
                                           in_=gexp[:, br, :].rearrange("c (h t) -> c h t", t=TS),
                                           compare_op=ALU.not_equal, fill=1.0, base=-br,
                                           pattern=[[-3, G * R], [0, TS]], channel_multiplier=1))
            pc(nc.gpsimd.affine_select(out=cbias[:, :, :], in_=cbias[:, :, :], compare_op=ALU.is_ge, fill=NEG,
                                       base=1 - BLK, pattern=[[P, PT_TOK], [-BLK, PBLK]], channel_multiplier=1))
            pc.wait()
            pc(nc.gpsimd.affine_select(out=tri[:, :, :], in_=tri[:, :, :], compare_op=ALU.is_ge, fill=0.0,
                                       base=-1, pattern=[[TS, P // TS], [1, TS]], channel_multiplier=-1))
            pc.wait()
            pool.sem_inc(s_mask, 1)
            pool.wait_ge(s_gemm, 2 + S_OUT)
            pool.wait_ge(s_cmpv, 2 + NB)
            pc(nc.gpsimd.tensor_copy(cmp_t[:, :, :, :].rearrange("p b m n -> p (b m n)"),
                                     cmp_t0[:, :, :, :].rearrange("p b m n -> p (b m n)")))
            pc(nc.gpsimd.memset(wmask[:, :], 0.0))
            pc(nc.gpsimd.memset(causal[:, :], 0.0))
            pc.wait()
            pc(nc.gpsimd.affine_select(out=causal[:, :], in_=causal[:, :], compare_op=ALU.is_ge, fill=NEG,
                                       base=TP - P, pattern=[[-1, 2 * TP - P]], channel_multiplier=1))
            pc.wait()
            pool.sem_inc(s_mask, 1)

            def seq_q(h, i):
                pool.wait_ge(t_qk, 6 * h + 6 + 12 * i)
                nc.gpsimd.tensor_copy(sq_[h][:, :, :], qbd[:, bass.ds(2 * i + h, 1), :, :].rearrange("p b a n -> p (b a) n")).then_inc(t_qb, 1)

            def seq_gather(h, i):
                for hh in range(2):
                    pool.wait_ge(t_pv, 6 * h + 2 * hh + 2 + 12 * i)
                    nc.gpsimd.tensor_copy(idx1[2 * h + hh][:, :], idx[:, bass.ds(4 * i + 2 * h + hh, 1)]).then_inc(t_i, 1)
                    pool.wait_ge(t_i, 2 * h + hh + 1 + 4 * i)
                    pool.sem_inc(s_asked, 1)
                    nc.gpsimd.indirect_dma_start(
                        sg[2 * h + hh][:, :, :].rearrange("p j c -> p (j c)"), None, slc_rows,
                        bass.IndirectOffsetOnAxis(ap=idx1[2 * h + hh][:, 0:1], axis=0)).then_inc(s_sg[2 * h + hh], 16)

            pool.wait_ge(s_b, 10)
            seq_gather(0, 0)
            pool.wait_ge(s_pv, 2 + UNITS)
            pool.wait_ge(s_of, 2 + 2 * R)
            seq_q(0, 0)
            seq_q(1, 0)
            seq_gather(1, 0)
            with pool.Fori(1, NB // 2) as i:
                for h in range(2):
                    seq_q(h, i)
                    seq_gather(h, i)

        def split_hi(act, s, pairs=0):
            act.wait_ge(s_w[s % 2], raw_in(s, pairs))
            act.wait_ge(s_gemm, s + 1 + 2 * pairs)
            nc.scalar.activation(w_hi[s % 2][:, :], w_raw[s % 2][:, :], ACT.Copy).then_inc(s_hi, 1)

        def split_lo(dve, s, pairs=0):
            dve.wait_ge(s_hi, s + 1 + 2 * pairs)
            nc.vector.tensor_tensor(w_lo[s % 2][:, :], w_raw[s % 2][:, :], w_hi[s % 2][:, :].bitcast(F32),
                                    ALU.subtract).then_inc(s_lo, 1)

        def acc(s):
            return banks(2 * (s % 2), 2, TH)

        def y_copy(eng, n):
            q, t = n // (PT_TOK + 1), n % (PT_TOK + 1)
            rows = P if t < PT_TOK else TN
            eng.wait_ge(o_tr, n + 1)
            dst, src = o_rows[t][0:rows, q * 512:(q + 1) * 512], ps[0:rows, n % 8, :]
            if n % 2:
                nc.scalar.activation(dst, src, ACT.Copy).then_inc(o_cp[1], 1)
            else:
                nc.vector.tensor_copy(dst, src).then_inc(o_cp[0], 1)

        @block.scalar
        def _(act):
            split_hi(act, S_GATE)

            def x_parts_act(t, n, q):
                act.wait_ge(s_tr, 4 * t + q + 1)
                src = ps[:, q, :].rearrange("p (k c) -> p k c", c=P)[:, :, 0:n]
                cols = bass.ds(t * P, n)
                if q < 3:
                    nc.scalar.activation(x_t[:, 4 * q:4 * q + 4, cols], src, ACT.Copy).then_inc(s_xt, 1)
                nc.scalar.activation(x_hi[:, 4 * q:4 * q + 4, cols], src, ACT.Copy).then_inc(s_xhi, 1)

            with act.Fori(0, PT_TOK) as t:
                for q in range(4):
                    x_parts_act(t, P, q)
            for q in range(4):
                x_parts_act(PT_TOK, TN, q)
            split_hi(act, S_CONV)
            act.wait_ge(s_gate, 1)
            nc.scalar.activation(gates0[0:NG, :], gates0[0:NG, :], ACT.Sigmoid).then_inc(s_gate, 1)
            with act.Fori(0, (S_OUT - 2) // 2) as i:
                for u in range(2):
                    split_hi(act, 2 + u, i)
            split_hi(act, S_OUT - 1)

            for t in range(PT_TOK + 1):
                n = P if t < PT_TOK else TN
                act.wait_ge(s_kvT, t + 1)
                nc.scalar.activation(kvn[0:n, t, :].rearrange("p (b c) -> p b c", b=3), ps[0:n, 3 * (t % 2):3 * (t % 2) + 3, :], ACT.Copy).then_inc(s_kvn, 1)
            act.wait_ge(s_b, 3)
            nc.scalar.activation(sc[:, :, :], sc[:, :, :], ACT.Exp, scale=SCALE).then_inc(s_a, 1)
            act.wait_ge(s_b, 4)
            nc.scalar.activation(ss[:, :, :], ss[:, :, :], ACT.Exp).then_inc(s_a, 1)
            act.wait_ge(s_one, 7)
            nc.scalar.activation(pct[:, :], ps[:, 0, :], ACT.Copy).then_inc(s_a, 1)
            act.wait_ge(s_one, 9)
            nc.scalar.activation(pcts[:, :, :].rearrange("p b n -> p (b n)"), flat(5, NB * P, NBLK), ACT.Copy).then_inc(s_a, 1)
            act.wait_ge(s_one, 10)
            nc.scalar.activation(vcs[:, :, :, :].rearrange("p (c b) a n -> p c (b a n)", c=4), ps[0:NBLK, 0:4, :], ACT.Copy).then_inc(s_a, 1)
            act.wait_ge(s_zout, 32)
            for j in range(2 * R):
                act.wait_ge(s_one, 11 + j)
                nc.scalar.activation(mix[:, j, 0:TP], ps[:, j % 4, :], ACT.Copy).then_inc(s_a, 1)

            def p_exp(u, r):
                act.wait_ge(s_mx, u + 3 + 16 * r)
                st, n = pst[u % 4], (UNIT_TILE[u % 8] + 1) * P
                for br in range(2):
                    last = nc.scalar.activation(pS[u % 4][:, br, 0:n], pS[u % 4][:, br, 0:n], ACT.Exp,
                                                bias=st[:, 0, br:br + 1], accum_out=st[:, 1, br:br + 1])
                last.then_inc(s_ex, 1)

            def p_q(a, r):
                nc.scalar.activation(pq[a][:, :], q_t[:, bass.ds(r, 1), a, 0:TP].rearrange("p r t -> p (r t)"), ACT.Copy, scale=SCALE).then_inc(s_q, 1)

            def p_act(r, last):
                for u in range(16):
                    nk = UNIT_TILE[u % 8] + 1
                    act.wait_ge(s_pt_, u + 5 + 16 * r)
                    act.wait_ge(s_pv, u + 1 + 16 * r)
                    nc.scalar.activation(pT[u % 2][:, 0:2 * nk, :].rearrange("p x q -> p (x q)"), flat(4, 2 * nk * P), ACT.Copy).then_inc(s_pe, 1)
                    if u + 2 < 16 or not last:
                        p_exp(u + 2, r)
                    if u in (7, 13) and not last:
                        act.wait_ge(s_qk, 1 + (8 if u == 7 else 16) + 16 * r)
                        p_q(u // 13, r + 1)

            act.sem_inc(s_pe, 1)
            act.wait_ge(s_b, 10)
            p_q(0, 0)
            p_q(1, 0)
            p_exp(0, 0)
            p_exp(1, 0)
            with act.Fori(0, R - 1) as r:
                p_act(r, False)
            p_act(R - 1, True)

            def k_copy(h, i, c):
                act.wait_ge(t_kt, 5 * h + c + 1 + 10 * i)
                act.wait_ge(t_qk, 6 * h + (10, 11, 13, 14, 15)[c] + 12 * i)
                kp = (h + c) % 2
                nc.scalar.activation(kT[kp][:, :, :], banks(2 * kp, 2, 512), ACT.Copy).then_inc(t_ke, 1)

            def s_exp(h, i):
                act.wait_ge(t_mx, h + 1 + 2 * i)
                for br, (c0, c1) in enumerate(((0, PAST + TS), (PAST + TS, NS_COLS))):
                    last = nc.scalar.activation(sS[h][:, c0:c1], sS[h][:, c0:c1], ACT.Exp,
                                                bias=sst[h][:, 0, br:br + 1], accum_out=sst[h][:, 1, br:br + 1])
                    last.then_inc(t_ex, 1)

            def p_copy(h, i, g):
                act.wait_ge(t_pt, 12 + 6 * h + g + 1 + 12 * i)
                act.wait_ge(t_pv, 6 * h + g + 7 + 12 * i)
                bank = 5 + 2 * (g % 2)
                if g < 5:
                    nc.scalar.activation(sT[:, 4 * g:4 * g + 4, :].rearrange("p x q -> p (x q)"), ps[:, bank, :], ACT.Copy).then_inc(t_pe, 1)
                else:
                    nc.scalar.activation(sT[0:TS, 20:22, :].rearrange("p x q -> p (x q)"), ps[0:TS, bank, 0:2 * P], ACT.Copy).then_inc(t_pe, 1)

            def act_phase(k, p, place=None):
                for c, groups in enumerate(P_GROUPS_LAST if place == "last K" else P_GROUPS):
                    if k and c < 5:
                        k_copy(*k, c)
                    if p and c == 0 and place != "last P":
                        s_exp(*p)
                    if place == "last P" and c == 4:
                        split_hi(act, S_OUT)
                    for g in groups if p else ():
                        p_copy(*p, g)
                        if place == "last K" and g == 2:
                            s_exp(*k)

            act.sem_inc(t_ke, 2)
            act.sem_inc(t_pe, 2)
            act.wait_ge(s_pv, 2 + UNITS)
            act_phase((0, 0), None)
            with act.Fori(0, NB // 2 - 1) as i:
                act_phase((1, i), (0, i))
                act_phase((0, i + 1), (1, i))
            act_phase((1, NB // 2 - 1), (0, NB // 2 - 1), "last K")
            act_phase(None, (1, NB // 2 - 1), "last P")

            act.wait_ge(t_of, 1 + NB)
            with act.Fori(0, KT // 2) as i:
                for v in range(2):
                    k = bass.ds(2 * i + v, 1)
                    nc.scalar.activation(mix_hi[:, k, :], mix[:, k, :], ACT.Copy).then_inc(s_mhi, 1)
            split_hi(act, S_OUT + 1)
            with act.Fori(0, KT // 2 - 1) as i:
                for u in range(2):
                    split_hi(act, S_OUT + 2 + u, i)
            split_hi(act, S_MLP)
            split_hi(act, S_MLP + 1)

            def norm_act(turn, b0, split):
                with act.Fori(0, KT // 2) as i:
                    for v in range(2):
                        act.wait_ge(l_sub, KT * turn + v + 1 + 2 * i)
                        act.wait_ge(l_acc, KT * turn + v + 1 + 2 * i)
                        nc.scalar.activation(sqr[v][:, :], h_t[:, bass.ds(2 * i + v, 1), :].rearrange("p k t -> p (k t)"), ACT.Square).then_inc(l_sq, 1)
                act.wait_ge(l_eps, 2 * turn + 1)
                nc.scalar.activation(rstd[:, :], rstd[:, :], ACT.Sqrt).then_inc(l_sd, 1)
                with act.Fori(0, KT // 2) as i:
                    for v in range(2):
                        k = bass.ds(2 * i + v, 1)
                        act.wait_ge(l_mul, KT * turn + v + 1 + 2 * i)
                        bias = pars_t[:, bass.ds(b0 + 2 * i + v, 1)]
                        if split:
                            nc.scalar.activation(h_hi[:, k, :], h_t[:, k, :], ACT.Identity, bias=bias)
                        nc.scalar.activation(h_t[:, k, :], h_t[:, k, :], ACT.Identity, bias=bias).then_inc(l_aff, 1)

            norm_act(0, LN1B, True)

            def hidden_act(s, v, c, i):
                act.wait_ge(s_gemm, s + 3 + 16 * c + 2 * i)
                act.wait_ge(f_f, v + 1 + 8 * c + 2 * i)
                nc.scalar.activation(rl[v][:, :].rearrange("p (h t) -> p h t", h=2), acc(s), ACT.Relu).then_inc(f_rl, 1)
                act.wait_ge(f_f, 2 + v + 1 + 8 * c + 2 * i)
                nc.scalar.activation(f_hi[:, bass.ds(2 * i + v, 1), :], fs[v][:, :], ACT.Copy).then_inc(f_h, 1)

            def chunk_act(c, last):
                with act.Fori(0, CT // 2) as i:
                    for u in range(2):
                        hidden_act(S_MLP + u, u, c, i)
                        split_hi(act, S_MLP + u + 2, 8 * c + i)
                with act.Fori(0, CT // 2 - last) as i:
                    for u in range(2):
                        split_hi(act, S_MLP + CT + u + 2, 8 * c + i)

            with act.Fori(0, NCHUNK - 1) as c:
                chunk_act(c, 0)
            chunk_act(NCHUNK - 1, 1)

            norm_act(1, LN2B, False)
            for n in range(1, XU, 2):
                y_copy(act, n)

        @block.vector
        def _(dve):
            dc = Chain(dve, s_dve)
            dve.sem_inc(s_acc, 2)
            dve.sem_inc(s_gfree, 2)
            dve.sem_inc(s_cmpv, 2)
            dve.wait_ge(s_par, 7 * 16)
            dve.wait_ge(s_const, 1)
            dc(nc.vector.tensor_copy(pt_f[:, :], pt_i[:, :]))
            dc.wait()
            nc.vector.tensor_scalar(pt_f[:, :], pt_f[:, :], w_of[:, 0:1], None, ALU.subtract).then_inc(s_pt, 1)
            dve.wait_ge(s_pre, 1)
            nc.vector.tensor_scalar(idx[:, :], ps[:, 4, 0:NGATH], 16.0, p_of[:, 0:1], ALU.mult, ALU.add).then_inc(s_idx, 1)
            dve.wait_ge(s_pre, 2)
            dc(nc.vector.tensor_copy(pars_t[:, :], ps[:, 5, 0:88]))
            dc(nc.vector.tensor_copy(st_t[:, :, :, :].rearrange("p c b j -> p (c b j)"), ps[:, 6, 0:P]))
            dc(nc.vector.tensor_copy(wt[:, :, :].rearrange("p m l -> p (m l)"), ps[:, 7, 0:2 * BLK]))
            split_lo(dve, S_GATE)

            def x_lo_part(t, n, q):
                src = ps[:, q, :].rearrange("p (k c) -> p k c", c=P)[:, :, 0:n]
                cols = bass.ds(t * P, n)
                dve.wait_ge(s_xhi, 4 * t + q + 1)
                if q == 3:
                    nc.vector.tensor_copy(x_t[:, 4 * q:4 * q + 4, cols], src).then_inc(s_xtd, 1)
                nc.vector.tensor_tensor(x_lo[:, 4 * q:4 * q + 4, cols], src,
                                        x_hi[:, 4 * q:4 * q + 4, cols].bitcast(F32), ALU.subtract).then_inc(s_xlo, 1)

            with dve.Fori(0, PT_TOK) as t:
                for q in range(4):
                    x_lo_part(t, P, q)
            for q in range(4):
                x_lo_part(PT_TOK, TN, q)
            split_lo(dve, S_CONV)

            def pieces(s):
                a = acc(s)
                return [(a[:, 0, :], 0), (a[:, 1, 0:TP - TH], TH), (a[:, 1, TP - TH:TH], TP)]

            def done(s, it=0):
                dve.wait_ge(s_gemm, s + 3 + it)

            dve.wait_ge(s_xsave, 16)
            dve.wait_ge(s_xlo, XU)
            dc(nc.vector.memset(zpad[:, 0:2], 0.0))
            done(S_GATE)
            nc.vector.tensor_copy(gates0[0:NG, :].rearrange("p (h t) -> p h t", h=2), acc(S_GATE)[0:NG, :, :]).then_inc(s_gate, 1)
            dve.wait_ge(s_gate, 1)
            dve.sem_inc(s_acc, 1)

            def sample(ap, lo, n):
                return ap[:, 2 + TP:2 + TP + NB * (2 + TS)].rearrange("p (b t) -> p b t", b=NB)[:, :, lo:lo + n]

            def fir_sample():
                return fir[:, 2 + TP:2 + TP + NB * (2 + TS)].rearrange("p (b t) -> p b t", b=NB)[:, :, 0:TS]

            def conv_xin(s, it):
                done(s, it)
                dc(nc.vector.tensor_copy(xin[:, :].rearrange("p (h t) -> p h t", h=2), acc(s)))
                dc.wait()
                dve.sem_inc(s_acc, 1)

            def conv_z(s, it, c):
                done(s, it)
                for src, t0 in pieces(s):
                    if t0 < TP:
                        dc(nc.vector.tensor_tensor(zpad[:, 2 + t0:2 + t0 + src.shape[1]], src, xin[:, t0:t0 + src.shape[1]], ALU.mult))
                    else:
                        dc(nc.vector.tensor_tensor(sample(zpad, 2, TS), src.rearrange("p (b t) -> p b t", b=NB),
                                                   xin[:, TP:T].rearrange("p (b t) -> p b t", b=NB), ALU.mult))
                dc(nc.vector.tensor_copy(sample(zpad, 0, 2), st_t[:, bass.ds(c, 1), :, :].rearrange("p c b j -> p (c b) j")))
                dc.wait()
                dve.sem_inc(s_acc, 1)
                dc(nc.vector.tensor_copy(zlast[:, bass.ds(c, 1), 0:2].rearrange("p c j -> p (c j)"), zpad[:, TP:TP + 2]))
                dc(nc.vector.tensor_copy(zlast[:, bass.ds(c, 1), 2:2 + 2 * NB].rearrange("p c (b j) -> p (c b) j", b=NB), sample(zpad, TS, 2)))
                taps = [pars_t[:, bass.ds(CW + j * NCONV + c, 1)] for j in range(3)]
                dc(nc.vector.tensor_scalar(fir[:, 0:ZW - 2], zpad[:, 2:ZW], taps[2], None, ALU.mult))
                for j in range(2):
                    dc.wait()
                    dc(nc.vector.scalar_tensor_tensor(fir[:, 0:ZW - 2], zpad[:, j:j + ZW - 2], taps[j], fir[:, 0:ZW - 2], ALU.mult, ALU.add))

            def conv_y(s, it, c):
                done(s, it)
                dc.wait()
                out = mix[:, bass.ds(NCONV + c, 1), :].rearrange("p c t -> p (c t)")
                for src, t0 in pieces(s):
                    if t0 < TP:
                        dc(nc.vector.tensor_tensor(out[:, t0:t0 + src.shape[1]], src, fir[:, t0:t0 + src.shape[1]], ALU.mult))
                    else:
                        dc(nc.vector.tensor_tensor(out[:, TP:T].rearrange("p (b t) -> p b t", b=NB),
                                                   src.rearrange("p (b t) -> p b t", b=NB), fir_sample(), ALU.mult))
                dc.wait()
                dve.sem_inc(s_acc, 1)

            def compress(i, v):
                g = gath[v % 2]
                dve.wait_ge(s_gath[v % 2], 16 * (v // 2 + 1) + 32 * i)
                dc(times_cmp(nc.vector, v % 2, 0))
                dc.wait()
                dve.wait_ge(s_vmul, v + 1 + 4 * i)
                dve.wait_ge(s_sel, v + 1 + 4 * i)
                nc.vector.tensor_reduce(part[v % 2][:, :], g[:, :, :].rearrange("p j c -> p c j"), AX.X, ALU.add).then_inc(s_part, 1)
                dve.wait_ge(s_part, v + 1 + 4 * i)
                dve.sem_inc(s_gfree, 1)

            def keep_cmp(i, h):
                dve.wait_ge(s_sel, 2 + 2 * h + 2 + 4 * i)
                nc.vector.tensor_copy(cmp_t0[:, bass.ds(2 * i + h, 1), :, :].rearrange("p b m n -> p (b m n)"),
                                      ps[:, 4 + h, 0:4 * NBLK]).then_inc(s_cmpv, 1)

            dve.wait_ge(s_wcmp, 32)
            split_lo(dve, S_CONV + 1)
            for i in dc.turns(NCONV // 2, 30):
                for u in range(6):
                    s, c = S_CONV + u, 2 * i + u // 3
                    if u % 3 == 0:
                        conv_xin(s, 6 * i)
                    elif u % 3 == 1:
                        conv_z(s, 6 * i, c)
                    else:
                        conv_y(s, 6 * i, c)
                    split_lo(dve, s + 2, 3 * i)
                    if u in (0, 1, 3, 4):
                        compress(i, (0, 1, None, 2, 3)[u])
                    if u == 3:
                        keep_cmp(i, 0)
                    if u == 5:
                        keep_cmp(i, 1)

            def keep(dst, s, it):
                done(s, it)
                nc.vector.tensor_copy(dst.rearrange("p (h t) -> p h t", h=2), acc(s)).then_inc(s_acc, 1)

            with dve.Fori(0, R) as r:
                for a in range(2):
                    keep(q_t[:, bass.ds(r, 1), a, :].rearrange("p r t -> p (r t)"), S_Q + a, 2 * r)
                    split_lo(dve, S_Q + a + 2, r)
            dve.wait_ge(s_zlT, 1)
            nc.vector.tensor_copy(zl_rows[:, :], flat(4, CONV, 2 + 2 * NB)).then_inc(s_zlv, 1)
            def keep_pair(i):
                for u in range(2):
                    keep(kv_t[:, bass.ds(2 * i + u, 1), :].rearrange("p r t -> p (r t)"), S_KV + u, 2 * i)
                    split_lo(dve, S_KV + u + 2, i)

            for m in range(2):
                keep_pair(m)
                dve.wait_ge(s_acc, 2 + S_KV + 2 * m + 2)
                rows = kv_t[:, KV_CMP + 2 * m:KV_CMP + 2 * m + 2, 0:TP].rearrange("p a (n l) -> p a n l", l=BLK)
                dc(nc.vector.tensor_tensor(tmp[:, :, :, :], rows, wt[:, m, :].unsqueeze(1).unsqueeze(1).broadcast_to([P, 2, PBLK, BLK]), ALU.mult))
                dc.wait()
                dc(nc.vector.tensor_reduce(kc[:, 2 * m:2 * m + 2, :], tmp[:, :, :, :], AX.X, ALU.add))
                dc.wait()
            with dve.Fori(2, NKV // 2 - 1) as i:
                keep_pair(i)
            keep(kv_t[:, NKV - 2, :], S_KV + NKV - 2, 0)
            keep(kv_t[:, NKV - 1, :], S_KV + NKV - 1, 0)
            dc(nc.vector.memset(qbd[:, :, :, :], 0.0))
            dve.wait_ge(s_mask, 1)
            dc(nc.vector.tensor_reduce(tok_of[:, :], ident[:, :].rearrange("p (x t) -> p t x", t=TS), AX.X, ALU.add))
            dc(nc.vector.tensor_reduce(grp_of[:, :], ident[:, :].rearrange("p (g x) -> p g x", g=G), AX.X, ALU.add))
            dc(nc.vector.tensor_reduce(pair_of[:, :], ident[:, :].rearrange("p (j n) -> p j n", n=PBLK), AX.X, ALU.add))
            dc(nc.vector.tensor_reduce(before[:, :], tri[:, :, :].rearrange("p x t -> p t x"), AX.X, ALU.add))
            dc(nc.vector.tensor_copy(e8[:, :].rearrange("n (x m) -> n x m", m=PBLK),
                                     ident[0:PBLK, 0:PBLK].unsqueeze(1).broadcast_to([PBLK, P // PBLK, PBLK])))
            dc.wait()
            for g in range(G):
                dc(nc.vector.tensor_scalar(same[:, g * 32:(g + 1) * 32].rearrange("p (r t) -> p r t", r=R),
                                           tok_of[:, :].unsqueeze(1).broadcast_to([P, R, TS]), grp_of[:, g:g + 1], None, ALU.mult))
            for m in range(2):
                dc(nc.vector.tensor_scalar(nmask[:, m, :], before[:, :], NEG, None, ALU.mult))
            for gl in range(2):
                half = slice(gl * HD, (gl + 1) * HD)
                dc(nc.vector.tensor_copy(kbd[half, :, gl * PBLK:(gl + 1) * PBLK], kc[half, 0:2, :]))
                for a in range(2):
                    g = 2 * a + gl
                    dc(nc.vector.tensor_scalar(qbd[half, :, a, g * 32:(g + 1) * 32].rearrange("p b (r t) -> p b r t", r=R),
                                               q_t[half, :, a, TP:T].rearrange("p r (b t) -> p b r t", b=NB), SCALE, None, ALU.mult))
            for m, kv in enumerate((KV_SLC, KV_WIN)):
                dc(nc.vector.tensor_copy(kn[:, m, :, :], kv_t[:, kv:kv + 2, TP:T]))
            dc.wait()
            dve.sem_inc(s_b, 1)
            dve.wait_ge(s_one, 1)
            dc(nc.vector.tensor_copy(gn[:, :, :].rearrange("p t c -> p (t c)"), ps[:, 6, 0:PT_TOK * NG]))
            dve.wait_ge(s_one, 2)
            dc(nc.vector.tensor_tensor(gtmp[:, :, :].rearrange("p m (b t) -> p (m b) t", t=TS),
                                       ps[:, 7, 0:3 * TN].rearrange("p (x t) -> p x t", t=TS),
                                       tok_of[:, :].unsqueeze(1).broadcast_to([P, 3 * NB, TS]), ALU.mult))
            dc.wait()
            dc(nc.vector.tensor_reduce(gs[:, :, :].rearrange("p m b -> p (m b)"),
                                       gtmp[:, :, :].rearrange("p m (b t) -> p (m b) t", t=TS), AX.X, ALU.add))
            dve.wait_ge(s_mask, 2)
            dc(nc.vector.tensor_scalar(wmask[:, :].rearrange("p (j c) -> p j c", j=4)[:, :, 0:2],
                                       before[:, :].rearrange("p (q j) -> p j q", j=4), -NEG, NEG, ALU.mult, ALU.add))
            dve.wait_ge(s_one, 3)
            nc.vector.tensor_copy(vcn[:, :], ps[0:PBLK, 0, 0:G * HD]).then_inc(s_b, 1)
            dve.wait_ge(s_one, 4)
            dc(nc.vector.tensor_tensor(sc[:, :, :].rearrange("p i (x n) -> p i x n", n=PBLK),
                                       ps[:, 1, :].rearrange("p (i x n) -> p i x n", i=PT_TOK, n=PBLK),
                                       cbias[:, :, :].unsqueeze(2).broadcast_to([P, PT_TOK, 16, PBLK]), ALU.add))
            dc.wait()
            heads = sc[:, :, :].rearrange("p i (x n) -> p (i x) n", n=PBLK)
            dc(nc.vector.tensor_reduce(st1[:, :], heads, AX.X, ALU.max))
            dc.wait()
            dc(nc.vector.tensor_scalar(st1[:, :], st1[:, :], NEG / 10, None, ALU.max))
            dc.wait()
            dve.wait_ge(s_b, 2)
            nc.vector.tensor_tensor(heads, heads, st1[:, :].unsqueeze(2).broadcast_to([P, PT_TOK * 16, PBLK]), ALU.subtract).then_inc(s_b, 1)
            dve.wait_ge(s_one, 5)
            seqs = ps[:, 2, 0:NB * NBLK].rearrange("p (b n) -> p b n", b=NB)
            dc(nc.vector.tensor_reduce(st3[:, :], seqs, AX.X, ALU.max))
            dc.wait()
            dve.wait_ge(s_b, 3)
            nc.vector.tensor_tensor(ss[:, :, :], seqs, st3[:, :].unsqueeze(2).broadcast_to([P, NB, NBLK]), ALU.subtract).then_inc(s_b, 1)
            dve.wait_ge(s_one, 6)
            for a in range(2):
                last = nc.vector.tensor_tensor(
                    vbd[:, a:2 * R:2, :].rearrange("p r (g d) -> p r g d", g=2),
                    ps[:, 3, a * P:(a + 1) * P].rearrange("p (g d) -> p g d", g=2).unsqueeze(1).broadcast_to([P, R, 2, HD]),
                    pair_of[:, :].rearrange("p (r a g) -> p a r g", a=2, g=2)[:, a].unsqueeze(3).broadcast_to([P, R, 2, HD]), ALU.mult)
            last.then_inc(s_b, 1)
            dve.wait_ge(s_a, 1)
            dc(nc.vector.tensor_reduce(st2[:, :], heads, AX.X, ALU.add))
            dc.wait()
            dc(nc.vector.tensor_scalar(st2[:, :], st2[:, :], 1e-30, None, ALU.max))
            dc.wait()
            dc(nc.vector.reciprocal(st2[:, :], st2[:, :]))
            dc.wait()
            for i in range(PT_TOK):
                dc(nc.vector.tensor_tensor(st1[:, i * 16:(i + 1) * 16].rearrange("p (r a g) -> p r a g", r=R, a=2),
                                           st2[:, i * 16:(i + 1) * 16].rearrange("p (r a g) -> p r a g", r=R, a=2),
                                           gn[:, i, :].rearrange("p (a g r m) -> p m r a g", a=2, g=2, r=R)[:, 0], ALU.mult))
            dc.wait()
            nc.vector.tensor_tensor(heads, heads, st1[:, :].unsqueeze(2).broadcast_to([P, PT_TOK * 16, PBLK]), ALU.mult).then_inc(s_b, 1)
            dve.wait_ge(s_a, 2)
            dc(nc.vector.tensor_reduce(st4[:, :], ss[:, :, :], AX.X, ALU.add))
            dc.wait()
            dc(nc.vector.reciprocal(st4[:, :], st4[:, :]))
            dc.wait()
            nc.vector.tensor_tensor(ss[:, :, :], ss[:, :, :], st4[:, :].unsqueeze(2).broadcast_to([P, NB, NBLK]), ALU.mult).then_inc(s_b, 1)
            dve.wait_ge(s_b, 7)
            nc.vector.tensor_tensor(pg[:, :, :], ss[:, :, :], gs[:, 0, :].unsqueeze(2).broadcast_to([P, NB, NBLK]), ALU.mult).then_inc(s_b, 1)
            dc(nc.vector.memset(vals[:, :, :], -1.0))
            dve.wait_ge(s_one, 8)
            dc.wait()
            dc(nc.vector.tensor_copy(vals[:, :, 1:NBLK - 1], ps[:, 4, 0:NB * NBLK].rearrange("p (b n) -> p b n", b=NB)[:, :, 1:NBLK - 1]))
            dc.wait()
            dve.sem_inc(s_b, 1)

            def each(op):
                for b in range(NB):
                    dc(op(b, vals[:, b, :]))
                dc.wait()

            each(lambda b, row: nc.vector.max(m8[:, b, :], row))
            each(lambda b, row: nc.vector.match_replace(row, m8[:, b, :], row, -2.0))
            each(lambda b, row: nc.vector.max(m5[:, b, :], row))
            dc(nc.vector.memset(m5[:, :, NSEL - FORCED - 8:8], -1.0))
            dc.wait()
            each(lambda b, row: nc.vector.match_replace(row, m5[:, b, :], row, -2.0))
            dc(nc.vector.tensor_scalar(mb[:, :, :], vals[:, :, 0:NBLK], -1.5, NEG, ALU.is_gt, ALU.mult))
            dc.wait()
            dc(nc.vector.memset(mb[:, :, 0:1], 0.0))
            dc(nc.vector.memset(mb[:, :, NBLK - 1:NBLK], 0.0))
            dve.wait_ge(s_one, 19)
            outs = flat(4, NB * P).rearrange("p (b a g x) -> p b a g x", b=NB, a=2, g=2)
            for gl in range(2):
                for a in range(2):
                    half = slice(gl * HD, (gl + 1) * HD)
                    dc(nc.vector.tensor_copy(mix[half, a:2 * R:2, TP:T].rearrange("p r (b t) -> p b r t", b=NB),
                                             outs[half, :, a, gl, :].rearrange("p b (r t) -> p b r t", r=R)))
            dve.wait_ge(s_a, 5 + 2 * R)
            dc.wait()
            dve.sem_inc(s_b, 1)

            def p_scores(u, r):
                st, n = pst[u % 4], (UNIT_TILE[u % 8] + 1) * P
                b0 = 2 * (u % 2)
                dve.wait_ge(s_qk, u + 2 + 16 * r)
                dve.wait_ge(s_pt_, u + 1 + 16 * r)
                dc(nc.vector.tensor_tensor(pS[u % 4][:, :, 0:n], banks(b0, 2, n),
                                           causal[:, TP - n:TP].unsqueeze(1).broadcast_to([P, 2, n]), ALU.add))
                dc.wait()
                nc.vector.tensor_reduce(st[:, 0, :], pS[u % 4][:, :, 0:n], AX.X, ALU.max, negate=True).then_inc(s_mx, 1)

            def p_scale(u, r):
                i, st, n = UNIT_TILE[u % 8], pst[u % 4], (UNIT_TILE[u % 8] + 1) * P
                g = 2 * (u // 8) + UNIT_HEAD[u % 8]
                dve.wait_ge(s_ex, u + 1 + 16 * r)
                dc(nc.vector.reciprocal(st[:, 2, :], st[:, 1, :]))
                dc.wait()
                dc(nc.vector.tensor_tensor(st[:, 2, :], st[:, 2, :], gn[:, i, bass.ds(g * 12 + r * 3 + 1, 2)], ALU.mult))
                dc.wait()
                for br in range(2):
                    last = nc.vector.tensor_scalar(pS[u % 4][:, br, 0:n], pS[u % 4][:, br, 0:n], st[:, 2, br:br + 1], None, ALU.mult)
                last.then_inc(s_sc, 1)

            def p_out(a, r):
                dve.wait_ge(s_pv, 8 * a + 7 + 3 + 16 * r)
                tile = mix[:, bass.ds(2 * r + a, 1), 0:TP].rearrange("p j t -> p (j t)")
                nc.vector.tensor_tensor(tile, tile, ps[:, 6 + a, :], ALU.add).then_inc(s_of, 1)

            dve.sem_inc(s_mx, 2)
            dve.sem_inc(s_of, 2)

            def p_dve(r, last):
                for u in range(16):
                    p_scale(u, r)
                    if u + 2 < 16 or not last:
                        p_scores(u + 2, r)
                    if u == 10:
                        p_out(0, r)
                p_out(1, r)

            p_scores(0, 0)
            p_scores(1, 0)
            for r in dc.turns(R - 1, 48):
                p_dve(r, False)
            p_dve(R - 1, True)

            def k_scores(h, i, c):
                dve.wait_ge(t_qk, 12 + 6 * h + c + 1 + 12 * i)
                if c == 0:
                    dve.wait_ge(t_pt, 6 * h + 6 + 12 * i)
                if c < 4:
                    hh = c // 2
                    bias = mb[:, bass.ds(2 * i + h, 1), hh * 16:(hh + 1) * 16].rearrange("p b n -> p (b n)")
                    ins = nc.vector.tensor_tensor(sS[h][:, c * 512:(c + 1) * 512].rearrange("p (j n s) -> p j n s", j=4, s=GROW),
                                                  ps[:, 4, :].rearrange("p (j n s) -> p j n s", j=4, s=GROW),
                                                  bias.unsqueeze(1).unsqueeze(3).broadcast_to([P, 4, 16, GROW]), ALU.add)
                elif c == 4:
                    ins = nc.vector.tensor_tensor(sS[h][:, PAST + TS:PAST + TS + WIN], ps[:, 4, :], wmask[:, :], ALU.add)
                else:
                    for m, at_ in enumerate((PAST, PAST + TS + WIN)):
                        ins = nc.vector.tensor_tensor(sS[h][:, at_:at_ + TS], ps[:, 4, m * TS:(m + 1) * TS], nmask[:, m, :], ALU.add)
                ins.then_inc(t_se, 1)

            def k_part_max(h, i, c):
                dve.wait_ge(t_se, 1 + 6 * h + c + 1 + 12 * i)
                parts = (((PAST, TS, 4), (PAST + TS + WIN, TS, 6)) if c == 5 else ((PAST + TS, WIN, 5),) if c == 4 else ((c * 512, 512, c),))
                for c0, n, slot in parts:
                    dc(nc.vector.tensor_reduce(smx[h][:, slot:slot + 1], sS[h][:, c0:c0 + n], AX.X, ALU.max))

            def k_max(h, i):
                dc.wait()
                for br, (c0, c1) in enumerate(((0, 5), (5, 7))):
                    last = nc.vector.tensor_reduce(sst[h][:, 0, br:br + 1], smx[h][:, c0:c1], AX.X, ALU.max, negate=True)
                last.then_inc(t_mx, 1)

            def s_scale(h, i):
                st = sst[h]
                for br in range(2):
                    dve.wait_ge(t_ex, 2 * h + br + 1 + 4 * i)
                    dc(nc.vector.reciprocal(st[:, 2, br:br + 1], st[:, 1, br:br + 1]))
                    dc.wait()
                    dc(nc.vector.tensor_tensor(st[:, 2, br:br + 1], st[:, 2, br:br + 1], gs[:, 1 + br, bass.ds(2 * i + h, 1)], ALU.mult))
                    dc.wait()
                    for c0 in (0, 512, 1024, 1536) if br == 0 else (PAST + TS,):
                        nc.vector.tensor_scalar(sS[h][:, c0:c0 + 512], sS[h][:, c0:c0 + 512], st[:, 2, br:br + 1], None, ALU.mult).then_inc(t_sc, 1)
                for br, c0 in enumerate((PAST, PAST + TS + WIN)):
                    last = nc.vector.tensor_scalar(sS[h][:, c0:c0 + TS], sS[h][:, c0:c0 + TS], st[:, 2, br:br + 1], None, ALU.mult)
                last.then_inc(t_sc, 1)

            def s_out_add(h, i):
                dve.wait_ge(t_pv, 12 + 6 * h + 6 + 12 * i)
                for gl in range(2):
                    half = slice(gl * HD, (gl + 1) * HD)
                    tile = mix[half, 0:2 * R, bass.ds(16 * i + TP + TS * h, TS)].rearrange("p (r a) t -> p a r t", a=2)
                    last = nc.vector.tensor_tensor(
                        tile, tile, ps[half, 6, 0:P].rearrange("p (a g r t) -> p g a r t", a=2, g=2, r=R)[:, gl], ALU.add)
                last.then_inc(t_of, 1)

            def dve_phase(k, p, place=None):
                for c in range(6 if k else 0):
                    k_scores(*k, c)
                    if p and c == 0:
                        s_scale(*p)
                    if c:
                        k_part_max(*k, c - 1)
                if k:
                    k_part_max(*k, 5)
                    k_max(*k)
                if place == "last K":
                    s_scale(*k)
                if place == "last P":
                    split_lo(dve, S_OUT)
                if p:
                    s_out_add(*p)

            dve.sem_inc(t_se, 1)
            dve.sem_inc(t_of, 1)
            dve.wait_ge(s_kvout, 16 * (3 * PT_TOK + 3))
            dve_phase((0, 0), None)
            for i in dc.turns(NB // 2 - 1, 22):
                dve_phase((1, i), (0, i))
                dve_phase((0, i + 1), (1, i))
            dve_phase((1, NB // 2 - 1), (0, NB // 2 - 1), "last K")
            dve_phase(None, (1, NB // 2 - 1), "last P")

            with dve.Fori(0, KT // 2) as i:
                for v in range(2):
                    k = bass.ds(2 * i + v, 1)
                    dve.wait_ge(s_mhi, v + 1 + 2 * i)
                    nc.vector.tensor_tensor(mix_lo[:, k, :], mix[:, k, :], mix_hi[:, k, :].bitcast(F32), ALU.subtract).then_inc(s_mlo, 1)
            split_lo(dve, S_OUT + 1)
            dve.wait_ge(s_xr, 16)

            def residual(s, i, u):
                done(s, 2 * i)
                k = bass.ds(2 * i + u, 1)
                nc.vector.scalar_tensor_tensor(h_t[:, k, :].rearrange("p k (h t) -> p (k h) t", h=2),
                                               x_r[:, k, :].rearrange("p k (h t) -> p (k h) t", h=2), ALPHA,
                                               acc(s), ALU.mult, ALU.add).then_inc(s_acc, 1)

            def clear_sum(turn):
                nc.vector.memset(h_sum[:, :], 0.0).then_inc(l_sum, 1)

            def add_up(s, it, turn, k):
                dve.wait_ge(s_acc, s + 3 + it)
                dve.wait_ge(l_sum, (KT + 1) * turn + 1 + k)
                nc.vector.tensor_tensor(h_sum[:, :], h_sum[:, :], h_t[:, bass.ds(k, 1), :].rearrange("p k t -> p (k t)"),
                                        ALU.add).then_inc(l_sum, 1)

            clear_sum(0)
            dve.wait_ge(s_mlo, KT)
            with dve.Fori(0, KT // 2) as i:
                for u in range(2):
                    residual(S_OUT + u, i, u)
                    add_up(S_OUT + u, 2 * i, 0, 2 * i + u)
                    split_lo(dve, S_OUT + u + 2, i)

            def norm_dve(turn, g0, split):
                dve.wait_ge(l_mean, turn + 1)
                with dve.Fori(0, KT // 2) as i:
                    for v in range(2):
                        k = bass.ds(2 * i + v, 1)
                        view = h_t[:, k, :].rearrange("p k (h t) -> p (k h) t", h=2)
                        nc.vector.tensor_tensor(view, view, banks(4, 2, TH), ALU.subtract).then_inc(l_sub, 1)
                dve.wait_ge(l_acc, 2 + KT * (turn + 1))
                nc.vector.tensor_scalar(rstd[:, :].rearrange("p (h t) -> p h t", h=2), banks(6, 2, TH), EPS, None, ALU.add).then_inc(l_eps, 1)
                dve.wait_ge(l_sd, turn + 1)
                nc.vector.reciprocal(rstd[:, :], rstd[:, :]).then_inc(l_eps, 1)
                dve.wait_ge(l_eps, 2 * turn + 2)

                def scale(k):
                    view = h_t[:, bass.ds(k, 1), :].rearrange("p k t -> p (k t)")
                    nc.vector.scalar_tensor_tensor(view, view, pars_t[:, bass.ds(g0 + k, 1)], rstd[:, :], ALU.mult, ALU.mult).then_inc(l_mul, 1)

                def low(k):
                    dve.wait_ge(l_aff, k + 1)
                    tile = bass.ds(k, 1)
                    nc.vector.tensor_tensor(h_lo[:, tile, :], h_t[:, tile, :], h_hi[:, tile, :].bitcast(F32), ALU.subtract).then_inc(l_lo, 1)

                scale(0)
                scale(1)
                with dve.Fori(0, KT // 2 - 1) as i:
                    for v in range(2):
                        scale(2 * i + v + 2)
                        if split:
                            low(2 * i + v)
                if split:
                    low(KT - 2)
                    low(KT - 1)

            norm_dve(0, LN1G, True)
            dve.sem_inc(f_f, 2)

            def hidden_dve(s, v, c, i):
                dve.wait_ge(f_rl, v + 1 + 8 * c + 2 * i)
                dve.wait_ge(f_l, v + 1 + 8 * c + 2 * i)
                nc.vector.scalar_tensor_tensor(fs[v][:, :].rearrange("p (h t) -> p h t", h=2), acc(s), 0.0,
                                               rl[v][:, :].rearrange("p (h t) -> p h t", h=2), ALU.max, ALU.mult).then_inc(f_f, 1)
                dve.wait_ge(f_f, 2 + v + 1 + 8 * c + 2 * i)
                dve.sem_inc(s_acc, 1)
                dve.wait_ge(f_h, v + 1 + 8 * c + 2 * i)
                nc.vector.tensor_tensor(f_lo[:, bass.ds(2 * i + v, 1), :].rearrange("p k t -> p (k t)"), fs[v][:, :],
                                        f_hi[:, bass.ds(2 * i + v, 1), :].rearrange("p k t -> p (k t)").bitcast(F32), ALU.subtract).then_inc(f_l, 1)

            def add_out(c, i, u, first):
                s = S_MLP + CT + u
                done(s, 16 * c + 2 * i)
                for j in range(2):
                    view = h_t[:, bass.ds(4 * i + 2 * u + j, 1), :].rearrange("p k (h t) -> p (k h) t", h=2)
                    part_ = banks(2 * (s % 2) + 4 * j, 2, TH)
                    if first:
                        ins = nc.vector.scalar_tensor_tensor(view, view, ALPHA, part_, ALU.mult, ALU.add)
                    else:
                        ins = nc.vector.tensor_tensor(view, view, part_, ALU.add)
                ins.then_inc(s_acc, 1)

            def chunk_dve(c, first=False, last=False):
                with dve.Fori(0, CT // 2) as i:
                    for u in range(2):
                        hidden_dve(S_MLP + u, u, c, i)
                        split_lo(dve, S_MLP + u + 2, 8 * c + i)
                if last:
                    clear_sum(1)
                with dve.Fori(0, CT // 2 - last) as i:
                    for u in range(2):
                        add_out(c, i, u, first)
                        split_lo(dve, S_MLP + CT + u + 2, 8 * c + i)
                        if last:
                            for j in range(2):
                                add_up(S_MLP + CT + u, 16 * c + 2 * i, 1, 4 * i + 2 * u + j)
                if last:
                    for u in range(2):
                        add_out(c, CT // 2 - 1, u, first)
                        for j in range(2):
                            add_up(S_MLP + CT + u, 16 * c + CT - 2, 1, KT - 4 + 2 * u + j)

            dve.sem_inc(f_l, 2)
            chunk_dve(0, first=True)
            with dve.Fori(1, NCHUNK - 1) as c:
                chunk_dve(c)
            chunk_dve(NCHUNK - 1, last=True)

            norm_dve(1, LN2G, False)
            for n in range(0, XU, 2):
                y_copy(dve, n)

        @block.tensor
        def _(pe):
            pe.sem_inc(s_gemm, 2)
            pe.sem_inc(s_sel, 2)
            pe.wait_ge(s_const, 1)
            pe.wait_ge(s_pt, 1)
            pe.wait_ge(s_wr, 64)
            nc.tensor.matmul(ps[:, 4, 0:NGATH], spread[:, :], pt_f[:, :], start=True, stop=True).then_inc(s_pre, 1)
            nc.tensor.transpose(ps[:, 5, 0:88], pars[:, :], ident[0:88, 0:88])
            for c in range(NCONV):
                last = nc.tensor.transpose(ps[:, 6, c * 16:(c + 1) * 16], st_in[:, c * P:(c + 1) * P], ident[0:2 * NB, 0:2 * NB])
            for m in range(2):
                last = nc.tensor.transpose(ps[:, 7, m * BLK:(m + 1) * BLK], w_rows[:, m * P:(m + 1) * P], ident[0:BLK, 0:BLK])
            last.then_inc(s_pre, 1)
            for t in range(PT_TOK + 1):
                n = P if t < PT_TOK else TN
                pe.wait_ge(s_x[t], 16)
                for q in range(4):
                    if t:
                        pe.wait_ge(s_xlo, 4 * (t - 1) + q + 1)
                    for k in range(4):
                        last = nc.tensor.transpose(ps[:, q, k * P:k * P + n], x_rows[0:n, t, (4 * q + k) * P:(4 * q + k + 1) * P], ident[0:n, 0:n])
                    last.then_inc(s_tr, 1)

            def gemm(s, it, acts, kts=KT, tiles=1, n=P, ready=None, before=0):
                pe.wait_ge(s_lo, s + 1 + it)
                pe.wait_ge(s_acc, s + 1 + it)
                hi, lo = w_hi[s % 2], w_lo[s % 2]
                a_hi, a_lo = acts
                for j in range(tiles):
                    out = banks(2 * (s % 2) + 4 * j, 2, TH)
                    for k in range(kts):
                        if ready is not None and j == 0:
                            pe.wait_ge(ready, before + k + 1)
                        at_ = (k * tiles + j) * n
                        for m, (w, x) in enumerate(((hi, a_hi), (hi, a_lo), (lo, a_hi))):
                            for h in range(2):
                                last = nc.tensor.matmul(out[:, h, :], w[:, at_:at_ + n], x[:, k, h * TH:(h + 1) * TH],
                                                        start=(k == 0 and m == 0), stop=(k == kts - 1 and m == 2))
                last.then_inc(s_gemm, 1)

            pe.wait_ge(s_xlo, XU)
            x_parts = (x_hi, x_lo)
            gemm(S_GATE, 0, x_parts)

            def sum_blocks(i, v):
                pe.wait_ge(s_part, v + 1 + 4 * i)
                if v % 2 == 0:
                    pe.wait_ge(s_cmpv, v // 2 + 1 + 2 * i)
                for m in range(4):
                    o = m * NBLK + (v % 2) * (NBLK // 2)
                    last = nc.tensor.matmul(ps[:, 4 + v // 2, o:o + NBLK // 2], part[v % 2][:, m * P:(m + 1) * P],
                                            sel8[:, :], start=True, stop=True)
                last.then_inc(s_sel, 1)

            with pe.Fori(0, NCONV // 2) as i:
                for u in range(6):
                    gemm(S_CONV + u, 6 * i, x_parts)
                    if u in (1, 2, 4, 5):
                        sum_blocks(i, (None, 0, 1, None, 2, 3)[u])
            with pe.Fori(0, R) as i:
                for u in range(2):
                    gemm(S_Q + u, 2 * i, x_parts)
            pe.wait_ge(s_cmpv, 2 + NB)
            for c in range(NCONV):
                last = nc.tensor.transpose(flat(4, CONV, 2 + 2 * NB)[:, c * P:(c + 1) * P], zlast[:, c, :], ident[:, :])
            last.then_inc(s_zlT, 1)
            with pe.Fori(0, NKV // 2) as i:
                for u in range(2):
                    gemm(S_KV + u, 2 * i, x_parts)

            pe.wait_ge(s_acc, 2 + S_OUT)
            pe.wait_ge(s_zlv, 1)
            for t in range(PT_TOK + 1):
                n = P if t < PT_TOK else TN
                if t >= 2:
                    pe.wait_ge(s_kvn, t - 1)
                for m in range(NKV):
                    last = nc.tensor.transpose(ps[0:n, 3 * (t % 2) + m // 4, (m % 4) * P:(m % 4 + 1) * P],
                                               kv_t[:, m, t * P:t * P + n], ident[:, :])
                last.then_inc(s_kvT, 1)
            pe.wait_ge(s_gate, 2)
            for t in range(PT_TOK):
                last = nc.tensor.transpose(ps[:, 6, t * NG:(t + 1) * NG], gates0[0:NG, t * P:(t + 1) * P], ident[0:NG, 0:NG])
            last.then_inc(s_one, 1)
            pe.wait_ge(s_mask, 1)
            for m in range(3):
                last = nc.tensor.matmul(ps[:, 7, m * TN:(m + 1) * TN], gexp[:, m, :], gates0[0:NG, TP:T], start=True, stop=True)
            last.then_inc(s_one, 1)
            pe.wait_ge(s_b, 1)
            pe.wait_ge(s_kvn, PT_TOK + 1)
            for a in range(2):
                last = nc.tensor.transpose(ps[0:PBLK, 0, a * P:(a + 1) * P], kc[:, 2 + a, :], ident[:, :])
            last.then_inc(s_one, 1)
            for i in range(PT_TOK):
                for r in range(R):
                    for a in range(2):
                        o = i * P + (2 * r + a) * 16
                        last = nc.tensor.matmul(ps[:, 1, o:o + 16], q_t[:, r, a, i * P:(i + 1) * P], kbd[:, a, :], start=True, stop=True)
            last.then_inc(s_one, 1)
            pe.wait_ge(s_mask, 2)
            for b in range(NB):
                for a in range(2):
                    last = nc.tensor.matmul(ps[:, 2, b * NBLK:(b + 1) * NBLK], qbd[:, b, a, :], cmp_t[:, b, a, :], start=(a == 0), stop=(a == 1))
            last.then_inc(s_one, 1)
            pe.wait_ge(s_b, 2)
            nc.tensor.matmul(ps[:, 3, 0:G * HD], e8[:, :], vcn[:, :], start=True, stop=True).then_inc(s_one, 1)
            pe.wait_ge(s_b, 6)
            for i in range(PT_TOK):
                last = nc.tensor.transpose(ps[:, 0, i * P:(i + 1) * P], sc[:, i, :], ident[:, :])
            last.then_inc(s_one, 1)
            pe.wait_ge(s_b, 7)
            nc.tensor.matmul(ps[:, 4, 0:NB * NBLK], same[:, :], ss[:, :, :].rearrange("p b n -> p (b n)"), start=True, stop=True).then_inc(s_one, 1)
            pe.wait_ge(s_b, 8)
            for b in range(NB):
                last = nc.tensor.transpose(flat(5, NB * P, NBLK)[:, b * P:(b + 1) * P], pg[:, b, :], ident[:, :])
            last.then_inc(s_one, 1)
            pe.wait_ge(s_a, 3)
            for b in range(NB):
                for a in range(2):
                    m = 2 * b + a
                    last = nc.tensor.transpose(ps[0:NBLK, m // 4, (m % 4) * P:(m % 4 + 1) * P], cmp_t[:, b, 2 + a, :], ident[:, :])
            last.then_inc(s_one, 1)
            for j in range(2 * R):
                pe.wait_ge(s_a, 5 + max(0, j - 3))
                nc.tensor.matmul(ps[:, j % 4, :], vbd[:, j, :], pct[:, :], start=True, stop=True).then_inc(s_one, 1)
            pe.wait_ge(s_b, 9)
            for b in range(NB):
                for a in range(2):
                    o = (2 * b + a) * HD
                    last = nc.tensor.matmul(flat(4, NB * P)[:, o:o + HD], vcs[:, b, a, :], pcts[:, b, a * HD:(a + 1) * HD], start=True, stop=True)
            last.then_inc(s_one, 1)

            def p_qk(u, r):
                a, gl, n = u // 8 % 2, UNIT_HEAD[u % 8], (UNIT_TILE[u % 8] + 1) * P
                half = slice(gl * HD, (gl + 1) * HD)
                if u % 8 == 0:
                    pe.wait_ge(s_q, u // 8 + 1 + 2 * r)
                pe.wait_ge(s_mx, u + 1 + 16 * r)
                for br, kv in enumerate((KV_SLC, KV_WIN)):
                    last = nc.tensor.matmul(ps[:, 2 * (u % 2) + br, 0:n], pq[a][half, n - P:n], kv_t[half, kv + a, 0:n], start=True, stop=True)
                last.then_inc(s_qk, 1)

            def p_turn(u, r):
                nk = UNIT_TILE[u % 8] + 1
                pe.wait_ge(s_sc, u + 1 + 16 * r)
                pe.wait_ge(s_pe, u + 1 + 16 * r)
                for x in range(2 * nk):
                    br, kt = x // nk, x % nk
                    last = nc.tensor.transpose(ps[:, 4 + x // 4, (x % 4) * P:(x % 4 + 1) * P], pS[u % 4][:, br, kt * P:(kt + 1) * P], ident[:, :])
                last.then_inc(s_pt_, 1)

            def p_pv(u, r):
                a, i, gl = u // 8, UNIT_TILE[u % 8], UNIT_HEAD[u % 8]
                nk = i + 1
                if u % 8 == 0:
                    pe.wait_ge(s_of, a + 1 + 2 * r)
                pe.wait_ge(s_pe, u + 2 + 16 * r)
                for x in range(2 * nk):
                    br, kt = x // nk, x % nk
                    v0 = ((KV_SLC, KV_WIN)[br] + 2 + a) * P + gl * HD
                    last = nc.tensor.matmul(ps[gl * HD:(gl + 1) * HD, 6 + a, i * P:(i + 1) * P], kvn[:, kt, v0:v0 + HD], pT[u % 2][:, x, :],
                                            start=(x == 0), stop=(x == 2 * nk - 1))
                last.then_inc(s_pv, 1)

            pe.wait_ge(s_b, 10)
            for first in (t_qk, t_pv, t_pt):
                pe.sem_inc(first, 12)
            pe.sem_inc(s_qk, 1)
            pe.sem_inc(s_pt_, 4)
            pe.sem_inc(s_pv, 2)

            def p_pe(r, last):
                for u in range(16):
                    if u + 2 < 16 or not last:
                        p_qk(u + 2, r)
                    if u:
                        p_pv(u - 1, r)
                    p_turn(u, r)
                p_pv(15, r)

            p_qk(0, 0)
            p_qk(1, 0)
            with pe.Fori(0, R - 1) as r:
                p_pe(r, False)
            p_pe(R - 1, True)

            def k_turn(h, i, c):
                pe.wait_ge(t_ke, 5 * h + c + 1 + 10 * i)
                if c in (0, 2):
                    pe.wait_ge(s_sg[2 * h + c // 2], 16 + 16 * i)
                if c == 4:
                    pe.wait_ge(s_wb[h], 16 + 16 * i)
                kp = (h + c) % 2
                for a in range(2):
                    for j in range(4):
                        src = sg[2 * h + c // 2][:, 4 * (c % 2) + j, a * P:(a + 1) * P] if c < 4 else wb[h][:, j, a * P:(a + 1) * P]
                        last = nc.tensor.transpose(ps[:, 2 * kp + a, j * P:(j + 1) * P], src, ident[:, :])
                last.then_inc(t_kt, 1)

            def k_qk(h, i, c):
                if c == 0:
                    pe.wait_ge(t_qb, h + 1 + 2 * i)
                if c < 5:
                    pe.wait_ge(t_ke, 5 * h + c + 3 + 10 * i)
                pe.wait_ge(t_se, 6 * h + c + 1 + 12 * i)
                for m in range(1 if c < 5 else 2):
                    for a in range(2):
                        if c < 5:
                            out, keys = ps[:, 4, :], kT[(h + c) % 2][:, a, :]
                        else:
                            out, keys = ps[:, 4, m * TS:(m + 1) * TS], kn[:, m, a, bass.ds(16 * i + TS * h, TS)]
                        last = nc.tensor.matmul(out, sq_[h][:, a, :], keys, start=(a == 0), stop=(a == 1))
                last.then_inc(t_qk, 1)

            def s_turn(h, i, g):
                pe.wait_ge(t_sc, 6 * h + g + 1 + 12 * i)
                pe.wait_ge(t_pe, 6 * h + g + 1 + 12 * i)
                bank = 5 + 2 * (g % 2)
                if g < 5:
                    for x in range(4):
                        c0 = (4 * g + x) * P + (TS if g == 4 else 0)
                        last = nc.tensor.transpose(ps[:, bank, x * P:(x + 1) * P], sS[h][:, c0:c0 + P], ident[:, :])
                else:
                    for m, c0 in enumerate((PAST, PAST + TS + WIN)):
                        last = nc.tensor.transpose(ps[0:TS, bank, m * P:(m + 1) * P], sS[h][:, c0:c0 + TS], ident[:, :])
                last.then_inc(t_pt, 1)

            def s_pvs(h, i, g):
                if g == 0:
                    pe.wait_ge(t_of, h + 1 + 2 * i)
                if g == 5:
                    pe.wait_ge(s_vn[h], 32 + 32 * i)
                pe.wait_ge(t_pe, 6 * h + g + 3 + 12 * i)
                for x in range(4 if g < 5 else 2):
                    for a in range(2):
                        cols = slice(G * HD + a * P, G * HD + (a + 1) * P)
                        if g < 4:
                            v, p = sg[2 * h + g // 2][:, 4 * (g % 2) + x, cols], sT[:, 4 * g + x, a * HD:(a + 1) * HD]
                        elif g == 4:
                            v, p = wb[h][:, x, cols], sT[:, 16 + x, a * HD:(a + 1) * HD]
                        else:
                            v, p = vn[h][:, x, a * P:(a + 1) * P], sT[0:TS, 20 + x, a * HD:(a + 1) * HD]
                        last = nc.tensor.matmul(ps[:, 6, a * HD:(a + 1) * HD], v, p, start=(g == 0 and x == 0 and a == 0),
                                                stop=(g == 5 and x == 1), skip_group_check=True)
                last.then_inc(t_pv, 1)

            def pe_phase(k, p, place=None):
                for c, groups in enumerate(P_GROUPS_LAST if place == "last K" else P_GROUPS):
                    if k and c < 5:
                        k_turn(*k, c)
                    if k and c:
                        k_qk(*k, c - 1)
                    if place == "last K" and c == 5:
                        k_qk(*k, 5)
                    for g in groups if p else ():
                        s_turn(*p, g)
                        if g:
                            s_pvs(*p, g - 1)
                if k and place != "last K":
                    k_qk(*k, 5)
                if p:
                    s_pvs(*p, 5)

            pe_phase((0, 0), None)
            with pe.Fori(0, NB // 2 - 1) as i:
                pe_phase((1, i), (0, i))
                pe_phase((0, i + 1), (1, i))
            pe_phase((1, NB // 2 - 1), (0, NB // 2 - 1), "last K")
            pe_phase(None, (1, NB // 2 - 1))

            for u in range(2):
                gemm(S_OUT + u, 0, (mix_hi, mix_lo), ready=s_mlo)
            with pe.Fori(1, KT // 2) as i:
                for u in range(2):
                    gemm(S_OUT + u, 2 * i, (mix_hi, mix_lo))

            def norm_pe(turn, steps):
                pe.wait_ge(s_acc, 2 + steps)
                pe.wait_ge(l_sum, (KT + 1) * (turn + 1))
                for h in range(2):
                    last = nc.tensor.matmul(ps[:, 4 + h, 0:TH], means[:, :], h_sum[:, h * TH:(h + 1) * TH], start=True, stop=True)
                last.then_inc(l_mean, 1)
                for k in range(KT):
                    pe.wait_ge(l_sq, KT * turn + k + 1)
                    for h in range(2):
                        last = nc.tensor.matmul(ps[:, 6 + h, 0:TH], means[:, :], sqr[k % 2][:, h * TH:(h + 1) * TH], start=(k == 0), stop=(k == KT - 1))
                    last.then_inc(l_acc, 1)

            pe.sem_inc(l_acc, 2)
            norm_pe(0, S_MLP)

            def chunk_pe(c, first=False):
                if first:
                    for u in range(2):
                        gemm(S_MLP + u, 0, (h_hi, h_lo), ready=l_lo)
                with pe.Fori(1 if first else 0, CT // 2) as i:
                    for u in range(2):
                        gemm(S_MLP + u, 16 * c + 2 * i, (h_hi, h_lo))
                hidden = dict(acts=(f_hi, f_lo), kts=CT, tiles=2)
                gemm(S_MLP + CT, 16 * c, ready=f_l, before=2 + CT * c, **hidden)
                gemm(S_MLP + CT + 1, 16 * c, **hidden)
                with pe.Fori(1, CT // 2) as i:
                    for u in range(2):
                        gemm(S_MLP + CT + u, 16 * c + 2 * i, **hidden)

            chunk_pe(0, first=True)
            with pe.Fori(1, NCHUNK) as c:
                chunk_pe(c)
            norm_pe(1, END)
            for q in range(4):
                pe.wait_ge(l_aff, KT + 4 * q + 4)
                for t in range(PT_TOK + 1):
                    n, rows = (PT_TOK + 1) * q + t, P if t < PT_TOK else TN
                    if n >= 8:
                        pe.wait_ge(o_cp[n % 2], (n - 8) // 2 + 1)
                    for k in range(4):
                        last = nc.tensor.transpose(ps[0:rows, n % 8, k * P:(k + 1) * P], h_t[:, 4 * q + k, t * P:t * P + rows], ident[:, :])
                    last.then_inc(o_tr, 1)


_INS = ["x_prompt", "x_sample", "cache_cmp", "cache_slc", "cache_win", "state_conv", "page_table", "w_in",
        "w_cmp_k", "w_cmp_v", "conv_w", "w_out", "ln1_g", "ln1_b", "w_mlp1", "w_mlp2", "ln2_g", "ln2_b"]
_OUTS = [(1, TP, D), (NB, TS, D), (1, 1, TP, 2, G, HD), (1, 1, TP, 2, G, HD), (1, 1, TP, 2, G, HD), (1, 1, 2, CONV),
         (1, NB, TS, 2, G, HD), (1, NB, TS, 2, G, HD), (1, NB, WIN, 2, G, HD), (1, NB, 2, CONV)]


def kernel(**inputs):
    import concourse.bacc as bacc
    from concourse.bass_utils import run_bass_kernel_spmd

    nc = bacc.Bacc("TRN2", target_bir_lowering=False, num_devices=1)
    arrays, args = {}, []
    for name in _INS:
        a = np.ascontiguousarray(inputs[name])
        arrays[f"in_{name}"] = a
        args.append(nc.dram_tensor(f"in_{name}", a.shape, mybir.dt.from_np(a.dtype), kind="ExternalInput").ap())
    for i, shape in enumerate(_OUTS):
        args.append(nc.dram_tensor(f"out_{i}", shape, F32, kind="ExternalOutput").ap())
    build(nc, *args)
    r = run_bass_kernel_spmd(nc, [arrays], core_ids=[0])
    return tuple(r.results[0][f"out_{i}"] for i in range(len(_OUTS)))
```
